# Optimizing a Trainium2 kernel written in Bass

```python
import math
import jax, jax.numpy as jnp
from jax import lax
import numpy as np

D_MODEL = 2048
BATCH = 1
SEQ = 256
DEPTH = 1

SSM_WIDTH = D_MODEL // 2
SSM_GROUP = 16
SSM_GROUPS = SSM_WIDTH // SSM_GROUP
SSM_STATE = 64
ATTN_WIDTH = D_MODEL - SSM_WIDTH
HEAD_DIM = 128
N_HEADS = ATTN_WIDTH // HEAD_DIM
DILATED_BRANCHES = ((128, 1), (512, 4), (2048, 16))
FFN_HIDDEN = ((8 * D_MODEL + 3 * 256 - 1) // (3 * 256)) * 256
IN_PROJ_WIDTH = SSM_WIDTH + 3 * ATTN_WIDTH
N_MOD = 6
DT_MIN = 1e-3
DT_MAX = 1e-1
NORM_EPS = 1e-6
MASK_VALUE = -1e30


def _rms(x, w):
    xf = x.astype(jnp.float32)
    y = xf * lax.rsqrt(jnp.mean(xf * xf, axis=-1, keepdims=True) + NORM_EPS)
    return y * w.astype(jnp.float32)

def _modulate(y, shift, scale):
    return y * (1.0 + scale.astype(jnp.float32)[:, None, :]) + shift.astype(jnp.float32)[:, None, :]

def _complex_linear_combine(e1, e2):
    a1r, a1i, b1r, b1i = e1
    a2r, a2i, b2r, b2i = e2
    ar = a1r * a2r - a1i * a2i
    ai = a1r * a2i + a1i * a2r
    br = a2r * b1r - a2i * b1i + b2r
    bi = a2r * b1i + a2i * b1r + b2i
    return ar, ai, br, bi

def _s5_mixer(u, a_re, a_im, log_dt, b_re, b_im, c_re, c_im, d, w_glu):
    B, S, _ = u.shape
    f32 = jnp.float32
    uf = u.astype(f32).reshape(B, S, SSM_GROUPS, SSM_GROUP)
    a_re = a_re.astype(f32)
    a_im = a_im.astype(f32)
    dt = jnp.exp(log_dt.astype(f32))[:, None]
    mag = jnp.exp(a_re * dt)
    abar_re = mag * jnp.cos(a_im * dt)
    abar_im = mag * jnp.sin(a_im * dt)
    num_re = abar_re - 1.0
    num_im = abar_im
    den = a_re * a_re + a_im * a_im
    z_re = (num_re * a_re + num_im * a_im) / den
    z_im = (num_im * a_re - num_re * a_im) / den
    b_re = b_re.astype(f32)
    b_im = b_im.astype(f32)
    bbar_re = z_re[..., None] * b_re - z_im[..., None] * b_im
    bbar_im = z_re[..., None] * b_im + z_im[..., None] * b_re
    bu_re = jnp.einsum('bsgc,gnc->sbgn', uf, bbar_re)
    bu_im = jnp.einsum('bsgc,gnc->sbgn', uf, bbar_im)
    a_seq_re = jnp.broadcast_to(abar_re[None, None], (S, 1, SSM_GROUPS, SSM_STATE))
    a_seq_im = jnp.broadcast_to(abar_im[None, None], (S, 1, SSM_GROUPS, SSM_STATE))
    _, _, h_re, h_im = lax.associative_scan(
        _complex_linear_combine, (a_seq_re, a_seq_im, bu_re, bu_im), axis=0)
    y = (jnp.einsum('sbgn,gcn->bsgc', h_re, c_re.astype(f32))
         - jnp.einsum('sbgn,gcn->bsgc', h_im, c_im.astype(f32))
         + d.astype(f32) * uf)
    y = jax.nn.gelu(y.reshape(B, S, SSM_WIDTH))
    return y * jax.nn.sigmoid(y @ w_glu.astype(f32))

def _dilated_branch(q, k, v, slopes, window, dilation):
    B, S, H, E = q.shape
    blk = window // dilation
    span = blk * dilation
    s_pad = ((S + span - 1) // span) * span
    pad = s_pad - S
    L = s_pad // dilation
    nb = L // blk

    def strided_blocks(t):
        t = jnp.pad(t, ((0, 0), (0, pad), (0, 0), (0, 0)))
        t = t.reshape(B, L, dilation, H, E).transpose(0, 2, 3, 1, 4)
        return t.reshape(B, dilation, H, nb, blk, E)

    qb, kb, vb = strided_blocks(q), strided_blocks(k), strided_blocks(v)

    def with_prev(t):
        prev = jnp.concatenate([jnp.zeros_like(t[:, :, :, :1]), t[:, :, :, :-1]], axis=3)
        return jnp.concatenate([prev, t], axis=4)

    kc, vc = with_prev(kb), with_prev(vb)
    scores = jnp.einsum('bdhnqe,bdhnke->bdhnqk', qb, kc)
    qi = jnp.arange(blk)[:, None]
    ki = jnp.arange(2 * blk)[None, :]
    dist = qi + blk - ki
    band = (dist >= 0) & (dist <= blk)
    first = (jnp.arange(nb) == 0)[:, None, None]
    valid = band[None] & ~(first & (ki < blk)[None])
    bias = -slopes[:, None, None, None] * (dilation * dist).astype(jnp.float32)[None, None]
    scores = jnp.where(valid, scores + bias, MASK_VALUE)
    m = jnp.max(scores, axis=-1)
    p = jnp.exp(scores - m[..., None])
    l = jnp.sum(p, axis=-1)
    o = jnp.einsum('bdhnqk,bdhnke->bdhnqe', p, vc)

    m = m.reshape(B, dilation, H, L).transpose(0, 3, 1, 2).reshape(B, s_pad, H)[:, :S]
    l = l.reshape(B, dilation, H, L).transpose(0, 3, 1, 2).reshape(B, s_pad, H)[:, :S]
    o = o.reshape(B, dilation, H, L, E).transpose(0, 3, 1, 2, 4).reshape(B, s_pad, H, E)[:, :S]
    return m, l, o

def _dilated_attention(q, k, v, q_norm_w, k_norm_w):
    B, S, _ = q.shape
    q = _rms(q.reshape(B, S, N_HEADS, HEAD_DIM), q_norm_w) * (HEAD_DIM ** -0.5)
    k = _rms(k.reshape(B, S, N_HEADS, HEAD_DIM), k_norm_w)
    v = v.astype(jnp.float32).reshape(B, S, N_HEADS, HEAD_DIM)
    slopes = jnp.exp2(-8.0 * jnp.arange(1, N_HEADS + 1, dtype=jnp.float32) / N_HEADS)
    outs = [_dilated_branch(q, k, v, slopes, w, dl) for (w, dl) in DILATED_BRANCHES]
    ms = jnp.stack([o[0] for o in outs])
    ls = jnp.stack([o[1] for o in outs])
    os_ = jnp.stack([o[2] for o in outs])
    w = jnp.exp(ms - jnp.max(ms, axis=0, keepdims=True))
    num = jnp.sum(w[..., None] * os_, axis=0)
    den = jnp.sum(w * ls, axis=0)
    return (num / den[..., None]).reshape(B, S, ATTN_WIDTH)

def first_inputs(seed: int = 0) -> dict:
    key = jax.random.key(seed)
    ks = jax.random.split(key, 24)
    f32 = jnp.float32
    nrm = lambda k, shape, s: jax.random.normal(k, shape, f32) * s
    D, G, N, C = D_MODEL, SSM_GROUPS, SSM_STATE, SSM_GROUP
    x = jax.random.normal(ks[0], (BATCH, SEQ, D), f32)
    c = jax.random.normal(ks[1], (BATCH, D), f32)
    w_ada = nrm(ks[2], (DEPTH, D, N_MOD * D), 0.5 * D ** -0.5)
    b_ada = nrm(ks[3], (DEPTH, N_MOD * D), 0.05)
    norm1_w = 1.0 + nrm(ks[4], (DEPTH, D), 0.02)
    w_in = nrm(ks[5], (DEPTH, D, IN_PROJ_WIDTH), D ** -0.5)
    ssm_a_re = -0.5 + nrm(ks[6], (DEPTH, G, N), 0.01)
    ssm_a_im = jnp.pi * jnp.arange(N, dtype=f32)[None, None, :] + nrm(ks[7], (DEPTH, G, N), 0.01)
    ssm_log_dt = jax.random.uniform(ks[8], (DEPTH, G), f32, math.log(DT_MIN), math.log(DT_MAX))
    ssm_b_re = nrm(ks[9], (DEPTH, G, N, C), (2 * C) ** -0.5)
    ssm_b_im = nrm(ks[10], (DEPTH, G, N, C), (2 * C) ** -0.5)
    ssm_c_re = nrm(ks[11], (DEPTH, G, C, N), (2 * N) ** -0.5)
    ssm_c_im = nrm(ks[12], (DEPTH, G, C, N), (2 * N) ** -0.5)
    ssm_d = nrm(ks[13], (DEPTH, G, C), 1.0)
    ssm_w_glu = nrm(ks[14], (DEPTH, SSM_WIDTH, SSM_WIDTH), SSM_WIDTH ** -0.5)
    q_norm_w = 1.0 + nrm(ks[15], (DEPTH, HEAD_DIM), 0.02)
    k_norm_w = 1.0 + nrm(ks[16], (DEPTH, HEAD_DIM), 0.02)
    w_out = nrm(ks[17], (DEPTH, D, D), D ** -0.5)
    norm2_w = 1.0 + nrm(ks[18], (DEPTH, D), 0.02)
    w_ffn_gate = nrm(ks[19], (DEPTH, D, FFN_HIDDEN), D ** -0.5)
    w_ffn_up = nrm(ks[20], (DEPTH, D, FFN_HIDDEN), D ** -0.5)
    w_ffn_down = nrm(ks[21], (DEPTH, FFN_HIDDEN, D), FFN_HIDDEN ** -0.5)
    return {"x": x, "c": c, "w_ada": w_ada, "b_ada": b_ada, "norm1_w": norm1_w,
            "w_in": w_in, "ssm_a_re": ssm_a_re, "ssm_a_im": ssm_a_im,
            "ssm_log_dt": ssm_log_dt, "ssm_b_re": ssm_b_re, "ssm_b_im": ssm_b_im,
            "ssm_c_re": ssm_c_re, "ssm_c_im": ssm_c_im, "ssm_d": ssm_d,
            "ssm_w_glu": ssm_w_glu, "q_norm_w": q_norm_w, "k_norm_w": k_norm_w,
            "w_out": w_out, "norm2_w": norm2_w, "w_ffn_gate": w_ffn_gate,
            "w_ffn_up": w_ffn_up, "w_ffn_down": w_ffn_down}

def first_block(x, c, w_ada, b_ada, norm1_w, w_in, ssm_a_re, ssm_a_im, ssm_log_dt,
              ssm_b_re, ssm_b_im, ssm_c_re, ssm_c_im, ssm_d, ssm_w_glu,
              q_norm_w, k_norm_w, w_out, norm2_w, w_ffn_gate, w_ffn_up, w_ffn_down):
    cond = jax.nn.silu(c)
    splits = [SSM_WIDTH, SSM_WIDTH + ATTN_WIDTH, SSM_WIDTH + 2 * ATTN_WIDTH]
    for i in range(DEPTH):
        mod = cond @ w_ada[i] + b_ada[i]
        shift1, scale1, gate1, shift2, scale2, gate2 = jnp.split(mod, N_MOD, axis=-1)

        h = _modulate(_rms(x, norm1_w[i]), shift1, scale1).astype(x.dtype)
        proj = h @ w_in[i]
        u, q, k, v = jnp.split(proj, splits, axis=-1)
        y_ssm = _s5_mixer(u, ssm_a_re[i], ssm_a_im[i], ssm_log_dt[i], ssm_b_re[i], ssm_b_im[i],
                          ssm_c_re[i], ssm_c_im[i], ssm_d[i], ssm_w_glu[i])
        y_att = _dilated_attention(q, k, v, q_norm_w[i], k_norm_w[i])
        mixed = jnp.concatenate([y_ssm, y_att], axis=-1).astype(x.dtype) @ w_out[i]
        x = x + gate1[:, None, :] * mixed

        h2 = _modulate(_rms(x, norm2_w[i]), shift2, scale2).astype(x.dtype)
        ffn = (jax.nn.silu(h2 @ w_ffn_gate[i]) * (h2 @ w_ffn_up[i])) @ w_ffn_down[i]
        x = x + gate2[:, None, :] * ffn
    return x


CHUNK = 64
N_META = 16
D_MIX = D_MODEL
D_POOL = D_MIX // 2
POOL_WINDOWS = (2, 4, 8, 16)
N_POOL_GROUPS = len(POOL_WINDOWS)
POOL_GROUP = D_POOL // N_POOL_GROUPS
D_ATT = D_MIX - D_POOL
N_HEADS_2 = D_ATT // HEAD_DIM
D_IN = D_POOL + 3 * D_ATT + N_HEADS_2
D_FF = ((8 * D_MODEL // 3 + 255) // 256) * 256
Q_BLOCK = 128
EPS = 1e-6


def rmsnorm(x, g):
    xf = x.astype(jnp.float32)
    y = xf * lax.rsqrt(jnp.mean(xf * xf, axis=-1, keepdims=True) + EPS)
    return (y * g.astype(jnp.float32)).astype(x.dtype)

def swiglu(x, w_gate, w_up, w_down):
    return (jax.nn.silu(x @ w_gate) * (x @ w_up)) @ w_down

def pool_mixer(p, pool_w, pool_scale):
    B, L, _ = p.shape
    pg = p.reshape(B, L, N_POOL_GROUPS, POOL_GROUP)
    c = jnp.cumsum(pg.astype(jnp.float32), axis=1)
    c = jnp.pad(c, ((0, 0), (1, 0), (0, 0), (0, 0)))
    win = jnp.array(POOL_WINDOWS, dtype=jnp.int32)
    end = jnp.arange(1, L + 1, dtype=jnp.int32)[:, None]
    start = jnp.maximum(end - win[None, :], 0)
    gidx = jnp.arange(N_POOL_GROUPS, dtype=jnp.int32)[None, :]
    window_sum = c[:, end, gidx] - c[:, start, gidx]
    count = (end - start).astype(jnp.float32)[None, :, :, None]
    pooled = (window_sum / count - pg.astype(jnp.float32)).astype(p.dtype)
    mixed = jnp.einsum('blgc,gcd->blgd', pooled, pool_w)
    return mixed.reshape(B, L, D_POOL) * pool_scale

def fox_attention(q, k, v, log_f):
    B, L, H, Dh = q.shape
    scale = 1.0 / np.sqrt(Dh).astype(np.float32)
    cum = jnp.cumsum(log_f, axis=-1)
    n_blocks = -(-L // Q_BLOCK)
    Lp = n_blocks * Q_BLOCK
    qp = jnp.pad(q, ((0, 0), (0, Lp - L), (0, 0), (0, 0)))
    cqp = jnp.pad(cum, ((0, 0), (0, 0), (0, Lp - L)))
    qb = qp.reshape(B, n_blocks, Q_BLOCK, H, Dh).transpose(1, 0, 2, 3, 4)
    cqb = cqp.reshape(B, H, n_blocks, Q_BLOCK).transpose(2, 0, 1, 3)
    kpos = jnp.arange(L, dtype=jnp.int32)

    def one_block(args):
        qi, cqi, bi = args
        qpos = bi * Q_BLOCK + jnp.arange(Q_BLOCK, dtype=jnp.int32)
        s = jnp.einsum('bqhd,bkhd->bhqk', qi, k).astype(jnp.float32) * scale
        s = s + (cqi[:, :, :, None] - cum[:, :, None, :])
        s = jnp.where(qpos[:, None] >= kpos[None, :], s, -jnp.inf)
        pr = jax.nn.softmax(s, axis=-1)
        return jnp.einsum('bhqk,bkhd->bqhd', pr.astype(v.dtype), v)

    out = lax.map(one_block, (qb, cqb, jnp.arange(n_blocks, dtype=jnp.int32)))
    out = out.transpose(1, 0, 2, 3, 4).reshape(B, Lp, H * Dh)
    return out[:, :L]

def second_inputs(seed: int = 0) -> dict:
    key = jax.random.key(seed)
    ks = jax.random.split(key, 20)
    f32 = jnp.float32

    def nrm(k, shape, s):
        return jax.random.normal(k, shape, f32) * s

    def gain(k, shape):
        return 1.0 + 0.05 * jax.random.normal(k, shape, f32)

    return {
        "x": jax.random.normal(ks[0], (BATCH, SEQ, D_MODEL), f32),
        "meta_tokens": nrm(ks[1], (N_META, D_MODEL), 1.0),
        "ffn1_norm": gain(ks[2], (DEPTH, D_MODEL)),
        "ffn1_w_gate": nrm(ks[3], (DEPTH, D_MODEL, D_FF), D_MODEL ** -0.5),
        "ffn1_w_up": nrm(ks[4], (DEPTH, D_MODEL, D_FF), D_MODEL ** -0.5),
        "ffn1_w_down": nrm(ks[5], (DEPTH, D_FF, D_MODEL), D_FF ** -0.5),
        "mix_norm": gain(ks[6], (DEPTH, D_MODEL)),
        "w_in": nrm(ks[7], (DEPTH, D_MODEL, D_IN), D_MODEL ** -0.5),
        "b_forget": jax.random.uniform(ks[8], (DEPTH, N_HEADS_2), f32, minval=1.0, maxval=5.0),
        "q_norm": gain(ks[9], (DEPTH, HEAD_DIM)),
        "k_norm": gain(ks[10], (DEPTH, HEAD_DIM)),
        "pool_w": nrm(ks[11], (DEPTH, N_POOL_GROUPS, POOL_GROUP, POOL_GROUP), POOL_GROUP ** -0.5),
        "pool_scale": 1.0 + 0.1 * jax.random.normal(ks[12], (DEPTH, D_POOL), f32),
        "w_out": nrm(ks[13], (DEPTH, D_MIX, D_MODEL), D_MIX ** -0.5),
        "ffn2_norm": gain(ks[14], (DEPTH, D_MODEL)),
        "ffn2_w_gate": nrm(ks[15], (DEPTH, D_MODEL, D_FF), D_MODEL ** -0.5),
        "ffn2_w_up": nrm(ks[16], (DEPTH, D_MODEL, D_FF), D_MODEL ** -0.5),
        "ffn2_w_down": nrm(ks[17], (DEPTH, D_FF, D_MODEL), D_FF ** -0.5),
    }

def second_block(x, meta_tokens, ffn1_norm, ffn1_w_gate, ffn1_w_up, ffn1_w_down, mix_norm, w_in,
              b_forget, q_norm, k_norm, pool_w, pool_scale, w_out, ffn2_norm, ffn2_w_gate,
              ffn2_w_up, ffn2_w_down):
    B = x.shape[0]
    meta = jnp.broadcast_to(meta_tokens[None].astype(x.dtype), (B, N_META, D_MODEL))
    h = jnp.concatenate([meta, x], axis=1)
    L = h.shape[1]
    for i in range(DEPTH):
        h = h + 0.5 * swiglu(rmsnorm(h, ffn1_norm[i]), ffn1_w_gate[i], ffn1_w_up[i], ffn1_w_down[i])

        u = rmsnorm(h, mix_norm[i])
        z = u @ w_in[i]
        o = D_POOL
        p = z[..., :o]
        q = z[..., o:o + D_ATT].reshape(B, L, N_HEADS_2, HEAD_DIM)
        k = z[..., o + D_ATT:o + 2 * D_ATT].reshape(B, L, N_HEADS_2, HEAD_DIM)
        v = z[..., o + 2 * D_ATT:o + 3 * D_ATT].reshape(B, L, N_HEADS_2, HEAD_DIM)
        f_logit = z[..., o + 3 * D_ATT:]

        pool_out = pool_mixer(p, pool_w[i], pool_scale[i])

        q = rmsnorm(q, q_norm[i])
        k = rmsnorm(k, k_norm[i])
        log_f = jax.nn.log_sigmoid(f_logit.astype(jnp.float32) + b_forget[i].astype(jnp.float32))
        att_out = fox_attention(q, k, v, log_f.transpose(0, 2, 1))

        mix = jnp.concatenate([pool_out, att_out.astype(pool_out.dtype)], axis=-1)
        h = h + mix @ w_out[i]

        h = h + 0.5 * swiglu(rmsnorm(h, ffn2_norm[i]), ffn2_w_gate[i], ffn2_w_up[i], ffn2_w_down[i])
    return h[:, N_META:]


def setup_inputs(seed=0):
    out = dict(first_inputs(seed))
    for name, value in second_inputs(seed + 1).items():
        if name != "x":
            out[name + "_2"] = value
    return out


def reference(
    x, c, w_ada, b_ada, norm1_w, w_in, ssm_a_re, ssm_a_im, ssm_log_dt, ssm_b_re, ssm_b_im,
    ssm_c_re, ssm_c_im, ssm_d, ssm_w_glu, q_norm_w, k_norm_w, w_out, norm2_w, w_ffn_gate,
    w_ffn_up, w_ffn_down, meta_tokens_2, ffn1_norm_2, ffn1_w_gate_2, ffn1_w_up_2, ffn1_w_down_2,
    mix_norm_2, w_in_2, b_forget_2, q_norm_2, k_norm_2, pool_w_2, pool_scale_2, w_out_2,
    ffn2_norm_2, ffn2_w_gate_2, ffn2_w_up_2, ffn2_w_down_2,
):
    x = first_block(
        x, c, w_ada, b_ada, norm1_w, w_in, ssm_a_re, ssm_a_im, ssm_log_dt, ssm_b_re, ssm_b_im,
        ssm_c_re, ssm_c_im, ssm_d, ssm_w_glu, q_norm_w, k_norm_w, w_out, norm2_w, w_ffn_gate,
        w_ffn_up, w_ffn_down,
    )
    return second_block(
        x, meta_tokens_2, ffn1_norm_2, ffn1_w_gate_2, ffn1_w_up_2, ffn1_w_down_2, mix_norm_2,
        w_in_2, b_forget_2, q_norm_2, k_norm_2, pool_w_2, pool_scale_2, w_out_2, ffn2_norm_2,
        ffn2_w_gate_2, ffn2_w_up_2, ffn2_w_down_2,
    )


_drawn_inputs = setup_inputs


def setup_inputs(seed=0):
    import zlib

    import numpy as np

    out = dict(_drawn_inputs(seed))
    spreads = {}
    factors = {'norm1_w': 8.0,
     'ssm_a_re': 64.0,
     'ssm_a_im': 64.0,
     'ssm_log_dt': 64.0,
     'ssm_b_re': 64.0,
     'ssm_b_im': 64.0,
     'ssm_c_re': 64.0,
     'ssm_c_im': 64.0,
     'q_norm_w': 8.0,
     'k_norm_w': 8.0,
     'norm2_w': 8.0,
     'ffn1_norm_2': 11.368,
     'q_norm_2': 128.667,
     'k_norm_2': 101.287,
     'ffn2_norm_2': 10.932,
     'mix_norm_2': 4.001,
     'b_forget_2': 33.024,
     'pool_scale_2': 8.0}
    for name, (base, spread) in spreads.items():
        noise = np.random.default_rng([zlib.crc32(name.encode()), seed]).standard_normal(out[name].shape)
        drawn = base * np.exp(spread * noise) if base else spread * noise
        out[name] = __import__('jax').numpy.asarray(drawn.astype(out[name].dtype))
    for name, factor in factors.items():
        out[name] = (out[name] * factor).astype(out[name].dtype)
    return out
```

```python
from contextlib import ExitStack

import numpy as np

import concourse.bass as bass
from concourse import mybir

F32 = mybir.dt.float32
F32R = mybir.dt.float32r
ALU = mybir.AluOpType
ACT = mybir.ActivationFunctionType
AX_X = mybir.AxisListType.X

P = 128
D = 2048
KT = D // P
QUADS = KT // 4
SEQ = 256
META = 16
T = META + SEQ
HALFW = D // 2
HEADS = HALFW // P
FF = 5632
GROUP = 512
CK = 4
RING = 4
PARTS = (4, 4, 3)
STATES = 64
SSM_TILES = 64 * STATES // P
EPS = 1e-6
MAGIC = 1.5 * 2.0 ** 23
TWO_PI = 6.2831850
HALF_PI = float(np.float32(np.pi / 2))
PI_A = 6.28125
PI_B = 0.00193500518798828125
PI_C = float(2 * np.pi - 6.28125 - 0.00193500518798828125)
SEQ_COLS = slice(META, T)

V_C, V_N1, V_N2, V_F1, V_MIX, V_F2, V_D, V_PS, V_QK = 0, 16, 32, 48, 64, 80, 96, 104, 112
V_ROWS = 116

C_IDENT, C_ONES, C_ONEHOT, C_END = 0, 128, 256, 256 + HEADS * HEADS


def constants():
    ident = np.eye(P, dtype=np.float32)
    onehot = np.tile(np.eye(HEADS, dtype=np.float32).reshape(1, -1), (P, 1))
    const = np.concatenate([ident, np.ones((P, P), np.float32), onehot], axis=1)
    steps = np.tile(np.arange(SEQ, dtype=np.float32), (P, 1))
    sel = np.zeros((HEADS, HEADS, P), np.float32)
    for h in range(HEADS):
        sel[h, h] = 1.0
    dist, mult, mask = [], [], []
    for qt in range(2):
        q = np.arange(P * qt, P * qt + P)[:, None]
        k = np.arange(P * (qt + 1))[None]
        d = q - k
        m = ((d >= 0) & (d <= 128)).astype(np.float32)
        m += (d >= 0) & (d % 4 == 0) & (d <= 512)
        m += (d >= 0) & (d % 16 == 0) & (d <= 2048)
        mult.append(m)
        dist.append(np.where(m > 0, d, 1e36).astype(np.float32))
        k2 = np.arange(META + P * (qt + 1))[None]
        mask.append(np.where(q + META >= k2, 0.0, -1e30).astype(np.float32))
    return {
        "const": const, "steps": steps, "sel": sel.reshape(HEADS, HEADS * P),
        "dilated": np.concatenate(dist + mult, axis=1), "causal": np.concatenate(mask, axis=1),
    }


class Phase:

    def __init__(self, tally, name, iters, groups, cpg, kind="split"):
        self.name, self.iters, self.groups, self.cpg, self.kind = name, iters, groups, cpg, kind
        self.body = groups * cpg
        self.n0 = tally["n"]
        self.s0 = tally["s"]
        self.a0 = tally["a"]
        self.g0 = tally["g"]
        chunks = iters * self.body
        tally["n"] += chunks
        tally["s" if kind == "split" else "a"] += chunks
        if kind == "split":
            tally["g"] += iters * groups
        self.s1, self.g1 = tally["s"], tally["g"]
        assert self.n0 % RING == 0 and self.body % RING == 0 and self.g0 % 2 == 0 and (groups % 2 == 0 or kind != "split")


def plan():
    tally = {"n": 0, "s": 0, "a": 0, "g": 0}
    ph = []

    def add(name, *a, **k):
        ph.append(Phase(tally, name, *a, **k))

    def ffn(name):
        for i, groups in enumerate(PARTS):
            add(f"{name}.up{i}", groups, 2, 4)
            if groups == 4:
                add(f"{name}.down{i}", 2, 2, 4)
            else:
                add(f"{name}.down{i}", 1, 4, groups)

    add("ada1", 8, 1, 4, kind="ada")
    add("w_in", 4, 2, 4)
    add("ada2", 8, 2, 4, kind="ada")
    add("glu", 1, 2, 2)
    add("w_out", 2, 2, 4)
    ffn("ffn1")
    ffn("ffn2")
    add("w_in_2", 4, 2, 4)
    add("w_out_2", 2, 2, 4)
    ffn("ffn3")
    return ph


def build(nc, a, out):
    phases = plan()
    byname = {p.name: p for p in phases}
    order = {p.name: i for i, p in enumerate(phases)}
    stack = ExitStack()
    with stack:
        base = nc.sbuf_base + (-nc.sbuf_base) % 64
        cursor = [base]
        slab_bytes = nc.sbuf_usable_end - base - 2048
        stack.enter_context(nc.sbuf_tensor("slab", [P, (slab_bytes // 4)], F32))

        def at(name, shape, dt=F32, offset=None):
            n = 4 * int(np.prod(shape[1:]))
            if offset is None:
                offset = cursor[0]
                cursor[0] += (n + 63) // 64 * 64
                assert cursor[0] <= base + slab_bytes, (name, cursor[0] - base, slab_bytes)
            return nc.alloc_sbuf_tensor_at(name, shape, dt, offset=offset)

        raw = [at(f"raw{i}", [P, CK, GROUP]) for i in range(RING)]
        w_hi = [at(f"w_hi{i}", [P, CK, GROUP], F32R) for i in range(2)]
        w_lo = [at(f"w_lo{i}", [P, CK, GROUP], F32R) for i in range(2)]
        res = at("res", [P, KT, T])
        act_at = cursor[0]
        act_hi = at("act_hi", [P, KT, T], F32R)
        act_lo = at("act_lo", [P, KT, T], F32R)
        hid_at = cursor[0]
        hid_hi = at("hid_hi", [P, KT, T], F32R)
        hid_lo = at("hid_lo", [P, KT, T], F32R)
        two_at = cursor[0]
        sig = at("sig", [P, 4, T])
        val = at("val", [P, 4, T])
        proj = at("proj", [P, 32, T])
        ssq = at("ssq", [P, QUADS, T])
        rstd = at("rstd", [P, T])
        rtmp = at("rtmp", [P, T])
        const = at("const", [P, C_END])
        vecs = at("vecs", [P, V_ROWS])
        mod = at("mod", [P, 96])
        bada = at("bada", [P, 96])
        gain = at("gain", [P, KT])
        cond = at("cond", [P, KT])
        half_pi = at("half_pi", [P, 1])
        qk_gain = at("qk_gain", [P, 4])
        ident = const[:, C_IDENT:C_IDENT + P]
        ones = const[:, C_ONES:C_ONES + P]

        def onehot(h):
            return const[:, C_ONEHOT + HEADS * h:C_ONEHOT + HEADS * (h + 1)]

        xin = at("xin", [P, 2, D], offset=hid_at)
        metain = at("metain", [META, D], offset=hid_at + 16384)
        vin = at("vin", [V_ROWS, P], offset=hid_at + 24576)
        badain = at("badain", [96, P], offset=hid_at + 24576 + 512)
        outb = at("outb", [P, 2, D], offset=hid_at)
        area = {"a": [hid_at + 17408, two_at + 8704], "b": [act_at, act_at + 34816]}

        def over(which, name, shape, dt=F32):
            n = (4 * int(np.prod(shape[1:])) + 63) // 64 * 64
            o = area[which][0]
            area[which][0] += n
            assert area[which][0] <= area[which][1], name
            return at(name, shape, dt, offset=o)

        bb = over("a", "bb", [P, 2, SSM_TILES, 16])
        c_nat = over("a", "c_nat", [P, 2, 8, STATES])
        cd = over("a", "cd", [P, 2, 2, STATES])
        ct = over("a", "ct", [P, 2, 4 * 160])
        ebuf = over("a", "ebuf", [P, 2, 4, 32])
        bt = over("a", "bt", [P, 2, P])
        par = over("a", "par", [P, 4, SSM_TILES])
        pc = over("a", "pc", [P, 2, 4])
        steps = over("a", "steps", [P, SEQ])
        ui = over("a", "ui", [P, SEQ])
        bnat_at = area["b"][0]
        fr = over("b", "fr", [P, 2, SEQ])
        kk = over("b", "kk", [P, 2, SEQ])
        cs = over("b", "cs", [P, 2, SEQ])
        sn = over("b", "sn", [P, 2, 2, SEQ])
        t1 = over("b", "t1", [P, 2, SEQ])
        t2 = over("b", "t2", [P, 2, SEQ])
        vv = over("b", "vv", [P, 2, SEQ])
        gg = over("b", "gg", [P, 2, SEQ])
        o1 = over("b", "o1", [P, 2, SEQ])
        o2 = over("b", "o2", [P, 2, SEQ])
        hh = over("b", "hh", [P, 2, 2, SEQ])
        b_nat = at("b_nat", [P, 2, SSM_TILES, 16], offset=bnat_at)
        b_tmp = at("b_tmp", [P, 2, SSM_TILES, 16], offset=bnat_at + 4096)
        pre = at("pre", [32, 18, P], offset=bnat_at + 8192)
        ldt = at("ldt", [32, 4], offset=bnat_at + 8192 + 18 * 512)
        area["m"] = [hid_at, two_at + 8704]
        sel = over("m", "sel", [HEADS, HEADS, P])
        vt = over("m", "vt", [P, 3, HEADS, P])
        unit_at = area["m"][0]
        lg = over("m", "lg", [P, 2, T])
        ex = over("m", "ex", [P, 2, T])
        pn = over("m", "pn", [P, 2, T])
        pt = over("m", "pt", [P, 2, 3 * P])
        area["m"][0] += 256
        win = at("win", [P, 2, 2, T], offset=unit_at)
        rq = at("rq", [HEADS, 5, T], offset=unit_at + 4352)
        st = over("m", "st", [P, 2, 4])
        pw_at = area["m"][0]
        pw = over("m", "pw", [P, 4, 2, 256])
        dil = at("dil", [P, 768], offset=pw_at)
        wf = over("m", "wf", [P, KT, HEADS])
        causal = over("m", "causal", [P, 416])
        fg = over("m", "fg", [HEADS, 4, T])
        bf = over("m", "bf", [HEADS, 1])
        cq = over("m", "cq", [P, 2, HEADS])
        sq = at("sq", [P, 2, T])
        pmix = at("pmix", [P, SEQ])

        ps = stack.enter_context(nc.psum_tensor("ps", [P, 8, 512], F32))

        def sem(name):
            return stack.enter_context(nc.semaphore(name))

        raw_landed = [sem(f"raw_landed{i}") for i in range(RING)]
        hi_ready, lo_ready, ada_done = sem("hi_ready"), sem("lo_ready"), sem("ada_done")
        chunk_done = sem("chunk_done")
        bank_free = [sem("bank_free_a"), sem("bank_free_b")]
        sig_ready, glu_mul, hid_step, hid_ready = sem("sig_ready"), sem("glu_mul"), sem("hid_step"), sem("hid_ready")
        act_ready = sem("act_ready")
        sq_ready, ssq_ready, ssq_sum = sem("sq_ready"), sem("ssq_ready"), sem("ssq_sum")
        ms_ready, root_ready, norm_val, norm_bias = sem("ms_ready"), sem("root_ready"), sem("norm_val"), sem("norm_bias")
        dve_link, act_link, pool_link = sem("dve_link"), sem("act_link"), sem("pool_link")
        const_in, vec_in, x_in, mix_in = sem("const_in"), sem("vec_in"), sem("x_in"), sem("mix_in")
        x_t, vec_t, vec_copied, cond_ready, mod_ready = sem("x_t"), sem("vec_t"), sem("vec_copied"), sem("cond_ready"), sem("mod_ready")
        res_in = sem("res_in")
        ssm_pre, par_t = sem("ssm_pre"), sem("par_t")
        ssm_tables, e_ready, bt_ps, bt_ready, ct_ps, ct_ready = (sem(n) for n in (
            "ssm_tables", "e_ready", "bt_ps", "bt_ready", "ct_ps", "ct_ready"))
        fr_step, fr_ready, tab_ready, bu_ready, rot_step, g_ready, pool_step, h_ready, y_mm, y_ready = (sem(n) for n in (
            "fr_step", "fr_ready", "tab_ready", "bu_ready", "rot_step", "g_ready", "pool_step", "h_ready", "y_mm", "y_ready"))
        pc_ready = sem("pc_ready")
        hs_sq, hs_mm, hs_ms, hs_root, hs_rstd, hs_bc, hs_done = (sem(n) for n in (
            "hs_sq", "hs_mm", "hs_ms", "hs_root", "hs_rstd", "hs_bc", "hs_done"))
        v_t, v_copied = sem("v_t"), sem("v_copied")
        score, logit, negmax, expd, wgt, p_norm, p_t, p_copied, pv, pv_hi, pv_free = (sem(n) for n in (
            "score", "logit", "negmax", "expd", "wgt", "p_norm", "p_t", "p_copied", "pv", "pv_hi", "pv_free"))
        ui_ready, tab_step, pre_act, pre_dve, e_free = (sem(n) for n in ("ui_ready", "tab_step", "pre_act", "pre_dve", "e_free"))
        gelu_done, y_split, pool_zero = sem("gelu_done"), sem("y_split"), sem("pool_zero")
        fg_mm, fg_step, cq_t, cq_ready = sem("fg_mm"), sem("fg_step"), sem("cq_t"), sem("cq_ready")
        pooled, pmm, pm_val, pm_hi, pm_free = sem("pooled"), sem("pmm"), sem("pm_val"), sem("pm_hi"), sem("pm_free")
        out_t, out_copied, out_done = sem("out_t"), sem("out_copied"), sem("out_done")

        def rows(w, r0, r1):
            return w[r0:r1, :].rearrange("(t p) n -> p t n", p=P)

        def source(name):
            if name in ("ada1", "ada2"):
                w, g0 = rows(a["w_ada"][0], 0, D), 0 if name == "ada1" else 8
                per = byname[name].groups
                return lambda it, j: w[:, CK * (j % 4):CK * (j % 4) + CK, bass.ds((g0 + j // 4) * GROUP + it * (per * GROUP), GROUP)]
            if name == "glu":
                w = rows(a["ssm_w_glu"][0], 0, HALFW)
                return lambda it, j: w[:, CK * (j % 2):CK * (j % 2) + CK, (j // 2) * GROUP:(j // 2) * GROUP + GROUP]
            if name in ("w_in", "w_out", "w_in_2", "w_out_2"):
                w = rows(a[name][0], 0, D)
                return lambda it, j: w[:, CK * (j % 4):CK * (j % 4) + CK, bass.ds((j // 4) * GROUP + it * (2 * GROUP), GROUP)]
            ffn, what = name.split(".")
            names = {"ffn1": ("w_ffn_gate", "w_ffn_up", "w_ffn_down"), "ffn2": ("ffn1_w_gate_2", "ffn1_w_up_2", "ffn1_w_down_2"),
                     "ffn3": ("ffn2_w_gate_2", "ffn2_w_up_2", "ffn2_w_down_2")}[ffn]
            part = int(what[-1])
            h0 = GROUP * sum(PARTS[:part])
            if what.startswith("up"):
                wg, wu = rows(a[names[0]][0], 0, D), rows(a[names[1]][0], 0, D)
                return lambda it, j: (wg if j < 4 else wu)[:, CK * (j % 4):CK * (j % 4) + CK, bass.ds(h0 + it * GROUP, GROUP)]
            w = rows(a[names[2]][0], h0, h0 + GROUP * PARTS[part])
            cpg = byname[name].cpg
            per = byname[name].groups
            return lambda it, j: w[:, CK * (j % cpg):CK * (j % cpg) + CK, bass.ds((j // cpg) * GROUP + it * (per * GROUP), GROUP)]

        def loop(eng, start, end, body):
            if end - start == 1:
                body(start)
            elif end > start:
                with eng.Fori(start, end) as i:
                    body(i)

        def stream(sp, name, head=True, rest=True):
            p = byname[name]
            src = source(name)
            prev = phases[order[name] - 1] if order[name] else None

            def body(it, first=False):
                for j in range(p.body):
                    if first and not (head if j < RING else rest):
                        continue
                    if not (first and j < RING):
                        if p.kind == "split":
                            sp.wait_ge(lo_ready, p.s0 + it * p.body + (j - RING + 1))
                        else:
                            sp.wait_ge(ada_done, p.a0 + it * p.body + (j - RING + 1))
                    elif prev is not None:
                        if prev.kind == "split":
                            sp.wait_ge(lo_ready, prev.s0 + prev.iters * prev.body - RING + j + 1)
                        else:
                            sp.wait_ge(ada_done, prev.a0 + prev.iters * prev.body - RING + j + 1)
                    sp.dma_start(raw[j % RING][:, :, :], src(it, j)).then_inc(raw_landed[j % RING], 16)

            body(0, True)
            if rest:
                loop(sp, 1, p.iters, body)

        def landed(eng, p, it, j):
            eng.wait_ge(raw_landed[j % RING], 16 * (p.n0 // RING + j // RING + 1) + it * (16 * p.body // RING))

        def split_hi(act, p, it, j):
            landed(act, p, it, j)
            if not (isinstance(it, int) and p.s0 + it * p.body + j < 2):
                act.wait_ge(chunk_done, p.s0 + it * p.body + j - 1)
            act.activation(w_hi[j % 2][:, :, :], raw[j % RING][:, :, :], ACT.Copy).then_inc(hi_ready, 1)

        def split_lo(dve, p, it, j):
            dve.wait_ge(hi_ready, p.s0 + it * p.body + j + 1)
            dve.tensor_tensor(w_lo[j % 2][:, :, :], raw[j % RING][:, :, :], w_hi[j % 2][:, :, :].bitcast(F32),
                              ALU.subtract).then_inc(lo_ready, 1)

        def run_phase(eng, name, split, evac, pending):
            p = byname[name]

            def body(it, first=False):
                for j in range(p.body):
                    split(eng, p, it, j)
                    if j % p.cpg == 1:
                        g = j // p.cpg
                        if g:
                            evac(p, it, g - 1)
                        elif first:
                            if pending:
                                pending()
                        else:
                            evac(p, it - 1, p.groups - 1)

            body(0, True)
            loop(eng, 1, p.iters, body)
            return lambda: evac(p, p.iters - 1, p.groups - 1)

        def group_done(eng, p, it, g):
            eng.wait_ge(chunk_done, p.s0 + it * p.body + (g + 1) * p.cpg)

        def group_index(p, it, g):
            return 1 + p.g0 // 2 + g // 2 + it * (p.groups // 2)

        def bank(half, cols):
            return ps[:, 4 * half:4 * half + 4, 0:cols.stop - cols.start]

        def counted(sem_, base_):
            return lambda c: (sem_, base_ + c + 1)

        def ada_chunk(pe, p, it, j, g, bank_):
            landed(pe, p, it, j)
            c = j % 4
            for t in range(CK):
                k = CK * c + t
                for m in range(4):
                    mm = pe.matmul(ps[:, bank_, bass.ds(4 * g + m, 1)], raw[j % RING][:, t, P * m:P * m + P], cond[:, k:k + 1],
                                   start=(k == 0 and m == 0), stop=(k == KT - 1), skip_group_check=True)
            mm.then_inc(ada_done, 1)

        def products(pe, name, hi, lo, cols, ready):
            p = byname[name]
            n = cols.stop - cols.start

            def body(it):
                for j in range(p.body):
                    g, c = divmod(j, p.cpg)
                    half = g % 2
                    if c == 0:
                        pe.wait_ge(bank_free[half], group_index(p, it, g))
                    if ready(c) is not None:
                        pe.wait_ge(*ready(c))
                    pe.wait_ge(lo_ready, p.s0 + it * p.body + j + 1)
                    for t in range(CK):
                        k = CK * c + t
                        for m in range(4):
                            o = ps[:, 4 * half + m, 0:n]
                            whi, wlo = w_hi[j % 2][:, t, P * m:P * m + P], w_lo[j % 2][:, t, P * m:P * m + P]
                            pe.matmul(o, whi, hi[:, k, cols], start=(k == 0), stop=False)
                            pe.matmul(o, whi, lo[:, k, cols], start=False, stop=False)
                            mm = pe.matmul(o, wlo, hi[:, k, cols], start=False, stop=(k == CK * p.cpg - 1))
                    mm.then_inc(chunk_done, 1)

            loop(pe, 0, p.iters, body)

        linked = {"dve": 0, "act": 0, "pool": 0}

        def link(eng, which, ins):
            s = {"dve": dve_link, "act": act_link, "pool": pool_link}[which]
            linked[which] += 1
            ins.then_inc(s, 1)
            eng.wait_ge(s, linked[which])

        NORMS = ["norm1", "norm2", "ffn1_2", "mix_2", "ffn2_2"]

        def norm_pe(pe, name):
            i = NORMS.index(name)
            for g in range(QUADS):
                pe.wait_ge(ssq_ready, QUADS * i + g + 1)
                mm = pe.matmul(ps[:, 0, 0:T], ones, ssq[:, g, :], start=(g == 0), stop=(g == QUADS - 1))
            mm.then_inc(ssq_sum, 1)

        def norm_act(act, name, shift=None):
            i = NORMS.index(name)
            act.wait_ge(ms_ready, i + 1)
            act.activation(rstd[:, :], rtmp[:, :], ACT.Sqrt).then_inc(root_ready, 1)
            if shift is not None:
                n = {"norm1": 0, "norm2": 1}[name]
                for q in range(QUADS):
                    v = (val, sig)[q % 2]
                    act.wait_ge(norm_val, QUADS * i + q + 1)
                    for t in range(4):
                        ins = act.activation(v[:, t, :], v[:, t, :], ACT.Identity,
                                             bias=mod[:, shift + 4 * q + t:shift + 4 * q + t + 1])
                    ins.then_inc(norm_bias, 1)

        def norm_dve(dve, name, weight, w0, shift=None):
            i = NORMS.index(name)
            dve.wait_ge(ssq_sum, i + 1)
            dve.tensor_scalar(rtmp[:, :], ps[:, 0, 0:T], 1.0 / D, EPS, ALU.mult, ALU.add).then_inc(ms_ready, 1)
            dve.wait_ge(root_ready, i + 1)
            link(dve, "dve", dve.reciprocal(rstd[:, :], rstd[:, :]))

            def scaled(q):
                v = (val, sig)[q % 2]
                if q >= 2:
                    dve.wait_ge(act_ready, ACT0[name] + q - 1)
                for t in range(4):
                    k = 4 * q + t
                    ins = dve.scalar_tensor_tensor(out=v[:, t, :], in0=res[:, k, :], scalar=weight[:, w0 + k:w0 + k + 1],
                                                   in1=rstd[:, :], op0=ALU.mult, op1=ALU.mult)
                ins.then_inc(norm_val, 1)

            scaled(0)
            for q in range(QUADS):
                if q + 1 < QUADS:
                    scaled(q + 1)
                v = (val, sig)[q % 2]
                s = slice(4 * q, 4 * q + 4)
                dve.wait_ge(norm_val, QUADS * i + q + 1)
                if shift is not None:
                    dve.wait_ge(norm_bias, QUADS * {"norm1": 0, "norm2": 1}[name] + q + 1)
                link(dve, "dve", dve.tensor_copy(act_hi[:, s, :], v[:, :, :]))
                dve.tensor_tensor(act_lo[:, s, :], v[:, :, :], act_hi[:, s, :].bitcast(F32), ALU.subtract).then_inc(act_ready, 1)

        ACT0 = {}
        total = 0
        for nm, k in (("norm1", 4), ("mix1", 2), ("norm2", 4), ("ffn1_2", 4), ("mix_2", 4), ("ffn2_2", 4)):
            ACT0[nm] = total
            total += k

        def squares_act(act, q, count, n):
            act.activation(sig[:, :, :], res[:, 4 * q:4 * q + 4, :] if isinstance(q, int) else
                           res[:, bass.ds(4 * q, 4), :], ACT.Square).then_inc(sq_ready, 1)

        def squares_dve(dve, q, count):
            dve.wait_ge(sq_ready, count + 1)
            o = ssq[:, q, :] if isinstance(q, int) else ssq[:, bass.ds(q, 1), :].rearrange("p a n -> p (a n)")
            dve.tensor_reduce(o, sig[:, :, :].rearrange("p t n -> p n t"), AX_X, ALU.add).then_inc(ssq_ready, 1)

        def copy_out(act, p, it, g):
            group_done(act, p, it, g)
            cols = SEQ_COLS if p.name == "w_in" else slice(0, T)
            dst = proj[:, 4 * g:4 * g + 4, cols] if isinstance(it, int) and it == 0 else \
                proj[:, bass.ds(it * (4 * p.groups) + 4 * g, 4), cols]
            act.activation(dst, bank(g % 2, cols), ACT.Copy).then_inc(bank_free[g % 2], 1)

        FFNS = ("ffn1", "ffn2", "ffn3")

        def hid0(p):
            f, what = p.name.split(".")
            return sum(PARTS) * FFNS.index(f) + sum(PARTS[:int(what[-1])])

        def ffn_cols(name):
            return slice(0, T) if name.startswith("ffn2") else SEQ_COLS

        def gate_act(act, p, it, g):
            if g == 0:
                cols = ffn_cols(p.name)
                q = hid0(p) + it
                group_done(act, p, it, 0)
                act.wait_ge(bank_free[1], group_index(p, it, 1))
                act.activation(sig[:, :, 0:cols.stop - cols.start], bank(0, cols), ACT.Silu).then_inc(bank_free[0], 1)

        def gate_dve(dve, p, it, g):
            if g == 1:
                cols = ffn_cols(p.name)
                n = cols.stop - cols.start
                q = hid0(p) + it
                group_done(dve, p, it, 1)
                dve.wait_ge(bank_free[0], group_index(p, it, 0) + 1)
                if not (isinstance(q, int) and q == 0):
                    dve.wait_ge(hid_ready, q)
                dve.tensor_tensor(val[:, :, 0:n], sig[:, :, 0:n], bank(1, cols), ALU.mult).then_inc(bank_free[1], 1)
                dve.wait_ge(bank_free[1], group_index(p, it, 1) + 1)
                hi = hid_hi[:, 0:4, cols] if isinstance(it, int) and it == 0 else hid_hi[:, bass.ds(4 * it, 4), cols]
                lo = hid_lo[:, 0:4, cols] if isinstance(it, int) and it == 0 else hid_lo[:, bass.ds(4 * it, 4), cols]
                dve.tensor_copy(hi, val[:, :, 0:n]).then_inc(hid_step, 1)
                dve.wait_ge(hid_step, q + 1)
                dve.tensor_tensor(lo, val[:, :, 0:n], hi.bitcast(F32), ALU.subtract).then_inc(hid_ready, 1)

        def tile_ap(buf, k, cols):
            return buf[:, k, cols] if isinstance(k, int) else buf[:, bass.ds(k, 1), cols].rearrange("p a n -> p (a n)")

        def add_dve(scale):
            def evac(dve, p, it, g):
                cols = ffn_cols(p.name) if p.name.startswith("ffn") else SEQ_COLS
                n = cols.stop - cols.start
                group_done(dve, p, it, g)
                for m in range(4):
                    k = 4 * g + m + it * (4 * p.groups)
                    r = tile_ap(res, k, cols)
                    s = scale[1] if scale[0] == "const" else (
                        mod[:, scale[1] + k:scale[1] + k + 1] if isinstance(k, int) else mod[:, bass.ds(scale[1] + k, 1)])
                    ins = dve.scalar_tensor_tensor(out=r, in0=ps[:, 4 * (g % 2) + m, 0:n], scalar=s, in1=r,
                                                   op0=ALU.mult, op1=ALU.add)
                ins.then_inc(bank_free[g % 2], 1)
            return evac

        def with_squares(count, evac):
            def both(dve, p, it, g):
                evac(dve, p, it, g)
                squares_dve(dve, g + it * p.groups, count + g + it * p.groups)
            return both

        def squares_of(count):
            def sq_act(act, p, it, g):
                act.wait_ge(bank_free[g % 2], group_index(p, it, g) + 1)
                q = g + it * p.groups
                if not (isinstance(q, int) and q == 0):
                    act.wait_ge(ssq_ready, count + q)
                squares_act(act, q, count, T)
            return sq_act

        def nothing(*_):
            pass

        def bind(eng, f):
            return lambda p, it, g: f(eng, p, it, g)

        def ffn_pe(pe, f, ready0):
            for i, groups in enumerate(PARTS):
                cols = ffn_cols(f)
                products(pe, f"{f}.up{i}", act_hi, act_lo, cols, counted(act_ready, ready0))
                products(pe, f"{f}.down{i}", hid_hi, hid_lo, cols, counted(hid_ready, hid0(byname[f"{f}.up{i}"])))

        def ffn_act(act, f, pending, last):
            for i in range(len(PARTS)):
                pending = run_phase(act, f"{f}.up{i}", split_hi, bind(act, gate_act), pending)
                e = last if i == len(PARTS) - 1 else nothing
                pending = run_phase(act, f"{f}.down{i}", split_hi, bind(act, e), pending)
            return pending

        def ffn_dve(dve, f, pending, evac, last):
            for i in range(len(PARTS)):
                pending = run_phase(dve, f"{f}.up{i}", split_lo, bind(dve, gate_dve), pending)
                up = pending

                def settle(up=up, p=byname[f"{f}.down{i}"]):
                    up()
                    if p.g0:
                        for h in range(2):
                            dve.wait_ge(bank_free[h], p.g0 // 2)
                pending = run_phase(dve, f"{f}.down{i}", split_lo, bind(dve, last if i == len(PARTS) - 1 else evac), settle)
            return pending

        block = nc.Block()
        with block:
            @block.sync
            def _(sp):
                sp.dma_start(vin[V_C:V_C + 16, :], a["c"].rearrange("a (t p) -> (a t) p", p=P)).then_inc(vec_in, 16)
                for row, nm in ((V_N1, "norm1_w"), (V_N2, "norm2_w"), (V_F1, "ffn1_norm_2"), (V_MIX, "mix_norm_2"), (V_F2, "ffn2_norm_2")):
                    sp.dma_start(vin[row:row + 16, :], a[nm].rearrange("a (t p) -> (a t) p", p=P)).then_inc(vec_in, 16)
                sp.dma_start(vin[V_D:V_D + 8, :], a["ssm_d"][0].rearrange("(t g) c -> t (g c)", t=8)).then_inc(vec_in, 16)
                sp.dma_start(vin[V_PS:V_PS + 8, :], a["pool_scale_2"].rearrange("a (t p) -> (a t) p", p=P)).then_inc(vec_in, 16)
                for i, nm in enumerate(("q_norm_w", "k_norm_w", "q_norm_2", "k_norm_2")):
                    sp.dma_start(vin[V_QK + i:V_QK + i + 1, :], a[nm]).then_inc(vec_in, 16)
                sp.dma_start(badain[:, :], a["b_ada"].rearrange("a (t p) -> (a t) p", p=P)).then_inc(vec_in, 16)
                stream(sp, "ada1")
                stream(sp, "w_in")
                stream(sp, "ada2", rest=False)
                sp.wait_ge(x_in, 32)

            @block.scalar
            def _(act):
                act.dma_start(const[:, :], a["const"]).then_inc(const_in, 16)
                act.dma_start(xin[:, :, :], a["x"][0].rearrange("(t p) n -> p t n", p=P)).then_inc(x_in, 16)
                act.dma_start(metain[:, :], a["meta_tokens_2"]).then_inc(x_in, 16)
                act.wait_ge(vec_t, 2)
                act.activation(vecs[:, :], ps[:, 7, 0:V_ROWS], ACT.Copy).then_inc(vec_copied, 1)
                act.wait_ge(vec_t, 2)
                act.activation(bada[:, :], ps[:, 7, P:P + 96], ACT.Copy).then_inc(vec_copied, 1)
                act.wait_ge(vec_copied, 1)
                act.activation(cond[:, :], vecs[:, V_C:V_C + 16], ACT.Silu).then_inc(cond_ready, 1)
                for q in range(QUADS):
                    act.wait_ge(x_t, q + 1)
                    b = 2 * (q % 2)
                    act.activation(res[:, 4 * q:4 * q + 4, SEQ_COLS],
                                   ps[:, b:b + 2, :].rearrange("p b (t n) -> p (b t) n", n=SEQ), ACT.Copy).then_inc(res_in, 1)
                act.wait_ge(x_t, QUADS + 1)
                act.activation(res[:, :, 0:META], ps[:, 6, 0:KT * META].rearrange("p (t n) -> p t n", n=META),
                               ACT.Copy).then_inc(res_in, 1)
                act.wait_ge(res_in, QUADS + 1)
                for q in range(QUADS):
                    if q:
                        act.wait_ge(ssq_ready, q)
                    squares_act(act, q, q, T)
                norm_act(act, "norm1", 0)
                flush = run_phase(act, "w_in", split_hi, bind(act, copy_out), None)
                flush()

            @block.vector
            def _(dve):
                for q in range(QUADS):
                    squares_dve(dve, q, q)
                dve.memset(half_pi[:, :], HALF_PI)
                dve.wait_ge(vec_copied, 2)
                scale = float(P) ** -0.5
                dve.tensor_scalar(qk_gain[:, 0:1], vecs[:, V_QK:V_QK + 1], scale, None, ALU.mult)
                dve.tensor_copy(qk_gain[:, 1:2], vecs[:, V_QK + 1:V_QK + 2])
                dve.tensor_scalar(qk_gain[:, 2:3], vecs[:, V_QK + 2:V_QK + 3], scale, None, ALU.mult)
                dve.tensor_copy(qk_gain[:, 3:4], vecs[:, V_QK + 3:V_QK + 4])
                dve.wait_ge(ada_done, 32)
                dve.tensor_tensor(mod[:, 0:32], ps[:, 5, 0:32], bada[:, 0:32], ALU.add).then_inc(bank_free[1], 1)
                dve.wait_ge(bank_free[1], 1)
                dve.tensor_scalar(gain[:, :], mod[:, 16:32], 1.0, None, ALU.add).then_inc(bank_free[0], 1)
                dve.wait_ge(bank_free[0], 1)
                link(dve, "dve", dve.tensor_tensor(gain[:, :], gain[:, :], vecs[:, V_N1:V_N1 + 16], ALU.mult))
                norm_dve(dve, "norm1", gain, 0, 0)
                flush = run_phase(dve, "w_in", split_lo, nothing, None)
                flush()

            @block.tensor
            def _(pe):
                pe.wait_ge(const_in, 16)
                pe.wait_ge(vec_in, 16 * 13)
                pe.transpose(ps[:, 7, 0:V_ROWS], vin[:, :], ident[0:V_ROWS, 0:V_ROWS]).then_inc(vec_t, 1)
                pe.transpose(ps[:, 7, P:P + 96], badain[:, :], ident[0:96, 0:96]).then_inc(vec_t, 1)
                pe.wait_ge(x_in, 32)
                for q in range(QUADS):
                    if q >= 2:
                        pe.wait_ge(res_in, q - 1)
                    for t in range(4):
                        for h in range(2):
                            mm = pe.transpose(ps[:, 2 * (q % 2) + t // 2, (t % 2) * SEQ + P * h:(t % 2) * SEQ + P * h + P],
                                              xin[:, h, P * (4 * q + t):P * (4 * q + t) + P], ident)
                    mm.then_inc(x_t, 1)
                for t in range(KT):
                    mm = pe.transpose(ps[:, 6, META * t:META * t + META], metain[:, P * t:P * t + P], ident[0:META, 0:META])
                mm.then_inc(x_t, 1)
                pe.wait_ge(cond_ready, 1)
                ada = byname["ada1"]

                def ada_body(it):
                    for j in range(4):
                        ada_chunk(pe, ada, it, j, it, 5)
                loop(pe, 0, ada.iters, ada_body)
                norm_pe(pe, "norm1")
                products(pe, "w_in", act_hi, act_lo, SEQ_COLS, counted(act_ready, ACT0["norm1"]))

        block = nc.Block()
        with block:
            SSM_IN = 16 * 8

            @block.sync
            def _(sp):
                for r, nm in enumerate(("ssm_a_re", "ssm_a_im")):
                    sp.dma_start(pre[:, r, :], a[nm][0].rearrange("(t g) n -> t (g n)", g=2)).then_inc(mix_in, 16)
                sp.dma_start(ldt[:, 0:2], a["ssm_log_dt"][0].rearrange("(t g) -> t g", g=2)).then_inc(mix_in, 16)
                sp.dma_start(steps[:, :], a["steps"]).then_inc(mix_in, 16)
                for r, nm in enumerate(("ssm_b_re", "ssm_b_im")):
                    sp.dma_start(b_nat[:, r, :, :], a[nm][0].rearrange("(t g) n c -> (g n) t c", g=2)).then_inc(mix_in, 16)
                for r, nm in enumerate(("ssm_c_re", "ssm_c_im")):
                    sp.dma_start(c_nat[:, r, :, :], a[nm][0].rearrange("(i g) c n -> (g c) i n", g=8)).then_inc(mix_in, 16)
                stream(sp, "ada2", head=False)
                stream(sp, "glu")

            @block.gpsimd
            def _(pool):
                pool.memset(ebuf[:, :, :, :], 0.0).then_inc(pool_zero, 1)
                pool.memset(ct[:, :, :], 0.0).then_inc(pool_zero, 1)

                def body(i):
                    for jj in range(4):
                        b, tile = jj % 2, 4 * i + jj
                        pool.wait_ge(g_ready, tile + 1)
                        g = gg[:, :, :]
                        if not (isinstance(tile, int) and tile == 0):
                            pool.wait_ge(h_ready, tile)
                        pool.tensor_tensor(o1[:, :, :], g, cs[:, b:b + 1, :].broadcast_to([P, 2, SEQ]), ALU.mult)
                        pool.tensor_tensor(o2[:, :, :], gg[:, ::-1, :], sn[:, b, :, :], ALU.mult).then_inc(pool_step, 1)
                        pool.wait_ge(pool_step, tile + 1)
                        if not (isinstance(tile, int) and tile < 2):
                            pool.wait_ge(y_mm, tile - 1)
                        pool.tensor_tensor(hh[:, b, :, :], o1[:, :, :], o2[:, :, :], ALU.subtract).then_inc(h_ready, 1)

                body(0)
                loop(pool, 1, 8, body)

            @block.scalar
            def _(act):
                act.wait_ge(mix_in, SSM_IN)
                act.activation(ldt[:, 2:4], ldt[:, 0:2], ACT.Exp).then_inc(pre_act, 1)
                act.wait_ge(pre_dve, 1)
                act.activation(pre[:, 3, :], pre[:, 2, :], ACT.Exp).then_inc(pre_act, 1)
                act.activation(pre[:, 4, :], pre[:, 2, :], ACT.Tanh, scale=0.5).then_inc(pre_act, 1)
                act.wait_ge(pre_dve, 9)
                act.activation(pre[:, 16, :], pre[:, 7, :], ACT.Abs).then_inc(pre_act, 1)
                act.activation(pre[:, 8, :], pre[:, 7, :], ACT.Sin, scale=TWO_PI).then_inc(pre_act, 1)
                act.activation(pre[:, 10, :], pre[:, 7, :], ACT.Sin, scale=TWO_PI / 2).then_inc(pre_act, 1)
                act.wait_ge(pre_act, 6)
                act.activation(pre[:, 9, :], pre[:, 16, :], ACT.Sin, scale=-TWO_PI, bias=half_pi[0:32, :]).then_inc(pre_act, 1)
                act.wait_ge(par_t, 1)
                act.activation(par[:, :, :], ps[:, 5, 0:P].rearrange("p (a t) -> p a t", a=4), ACT.Copy).then_inc(pre_act, 1)
                act.wait_ge(pool_zero, 2)
                act.wait_ge(pre_dve, 9 + 17 + 6)

                def tables(i, jj):
                    b, tile = jj % 2, 4 * i + jj
                    act.wait_ge(fr_ready, tile + 1)
                    if not (isinstance(tile, int) and tile < 2):
                        act.wait_ge(h_ready, tile - 1)
                    act.activation(sn[:, b, 0, :], fr[:, b, :], ACT.Sin, scale=TWO_PI)
                    act.activation(sn[:, b, 1, :], fr[:, b, :], ACT.Sin, scale=-TWO_PI)
                    act.activation(kk[:, b, :], fr[:, b, :], ACT.Abs).then_inc(tab_step, 1)
                    act.wait_ge(tab_step, tile + 1)
                    act.activation(cs[:, b, :], kk[:, b, :], ACT.Sin, scale=-TWO_PI, bias=half_pi[:, :]).then_inc(tab_ready, 1)

                def body(i):
                    four = bass.ds(4 * i, 4) if not isinstance(i, int) else slice(4 * i, 4 * i + 4)
                    one = bass.ds(i, 1) if not isinstance(i, int) else slice(i, i + 1)
                    for r in range(2):
                        act.activation(ebuf[0:64, r, :, 0:16], bb[0:64, r, four, :], ACT.Copy)
                        act.activation(ebuf[64:P, r, :, 16:32], bb[64:P, r, four, :], ACT.Copy)
                        for d in range(2):
                            ins = act.activation(cd[:, r, d, :], c_nat[:, r, one, :].rearrange("p a n -> p (a n)"), ACT.Copy)
                    ins.then_inc(e_ready, 1)
                    act.wait_ge(bt_ps, i + 1)
                    act.activation(bt[:, :, :], ps[:, 2, 0:2 * P].rearrange("p (a n) -> p a n", a=2), ACT.Copy).then_inc(bt_ready, 1)
                    act.wait_ge(ct_ps, i + 1)
                    for r in range(2):
                        for half in range(2):
                            rows_ = slice(64 * half, 64 * half + 64)
                            cols_ = slice(16 * half, 16 * half + 16)
                            dst = ct[rows_, r, :].rearrange("p (j q) -> p j q", q=160)[:, :, cols_]
                            src = ps[rows_, 3, P * r:P * r + P].rearrange("p (j q) -> p j q", q=32)[:, :, cols_]
                            ins = act.activation(dst, src, ACT.Copy, scale=(1.0, -1.0)[r])
                    ins.then_inc(ct_ready, 1)
                    for jj in range(4):
                        tables(i, jj)

                body(0)
                loop(act, 1, 8, body)
                act.wait_ge(y_ready, 8)
                for h in range(2):
                    act.activation(proj[:, 4 * h:4 * h + 4, SEQ_COLS], proj[:, 4 * h:4 * h + 4, SEQ_COLS],
                                   ACT.Gelu_apprx_tanh).then_inc(gelu_done, 1)

            @block.vector
            def _(dve):
                step = [0]

                def pstep(ins):
                    step[0] += 1
                    ins.then_inc(pre_dve, 1)
                    dve.wait_ge(pre_dve, step[0])

                def q(i):
                    return pre[:, i, :]

                def wide(x):
                    return x.rearrange("t (g o) -> t g o", o=1).broadcast_to([32, 2, STATES])

                dve.wait_ge(mix_in, SSM_IN)
                dve.wait_ge(pre_act, 1)
                pstep(dve.tensor_tensor(q(2).rearrange("t (g n) -> t g n", g=2), q(0).rearrange("t (g n) -> t g n", g=2), wide(ldt[:, 2:4]), ALU.mult))
                pstep(dve.tensor_tensor(q(5).rearrange("t (g n) -> t g n", g=2), q(1).rearrange("t (g n) -> t g n", g=2), wide(ldt[:, 2:4]), ALU.mult))
                pstep(dve.tensor_scalar(q(6), q(5), float(1 / (2 * np.pi)), MAGIC, ALU.mult, ALU.add))
                pstep(dve.tensor_scalar(q(6), q(6), -MAGIC, None, ALU.add))
                pstep(dve.scalar_tensor_tensor(out=q(7), in0=q(6), scalar=-PI_A, in1=q(5), op0=ALU.mult, op1=ALU.add))
                pstep(dve.scalar_tensor_tensor(out=q(7), in0=q(6), scalar=-PI_B, in1=q(7), op0=ALU.mult, op1=ALU.add))
                pstep(dve.scalar_tensor_tensor(out=q(7), in0=q(6), scalar=-PI_C, in1=q(7), op0=ALU.mult, op1=ALU.add))
                pstep(dve.tensor_scalar(q(7), q(7), float(1 / (2 * np.pi)), 0.5, ALU.mult, ALU.min))
                pstep(dve.tensor_scalar(q(7), q(7), -0.5, None, ALU.max))
                dve.wait_ge(pre_act, 7)
                pstep(dve.scalar_tensor_tensor(out=q(4), in0=q(3), scalar=1.0, in1=q(4), op0=ALU.add, op1=ALU.mult))
                pstep(dve.tensor_tensor(q(11), q(4), q(9), ALU.mult))
                pstep(dve.tensor_tensor(q(16), q(10), q(10), ALU.mult))
                pstep(dve.scalar_tensor_tensor(out=q(11), in0=q(16), scalar=-2.0, in1=q(11), op0=ALU.mult, op1=ALU.add))
                pstep(dve.tensor_tensor(q(12), q(3), q(8), ALU.mult))
                pstep(dve.tensor_tensor(q(13), q(0), q(0), ALU.mult))
                pstep(dve.tensor_tensor(q(17), q(1), q(1), ALU.mult))
                pstep(dve.tensor_tensor(q(13), q(13), q(17), ALU.add))
                pstep(dve.reciprocal(q(13), q(13)))
                pstep(dve.tensor_tensor(q(14), q(11), q(0), ALU.mult))
                pstep(dve.tensor_tensor(q(16), q(12), q(1), ALU.mult))
                pstep(dve.tensor_tensor(q(14), q(14), q(16), ALU.add))
                pstep(dve.tensor_tensor(q(14), q(14), q(13), ALU.mult))
                pstep(dve.tensor_tensor(q(15), q(12), q(0), ALU.mult))
                pstep(dve.tensor_tensor(q(16), q(11), q(1), ALU.mult))
                pstep(dve.tensor_tensor(q(15), q(15), q(16), ALU.subtract))
                pstep(dve.tensor_tensor(q(15), q(15), q(13), ALU.mult))
                dve.wait_ge(mix_in, SSM_IN)
                dve.wait_ge(pre_act, 8)

                def z(i):
                    return par[:, i, :].rearrange("p (t o) -> p t o", o=1).broadcast_to([P, SSM_TILES, 16])

                pstep(dve.tensor_tensor(b_tmp[:, 0, :, :], b_nat[:, 0, :, :], z(2), ALU.mult))
                pstep(dve.tensor_tensor(b_tmp[:, 1, :, :], b_nat[:, 1, :, :], z(3), ALU.mult))
                pstep(dve.tensor_tensor(bb[:, 0, :, :], b_tmp[:, 0, :, :], b_tmp[:, 1, :, :], ALU.subtract))
                pstep(dve.tensor_tensor(b_tmp[:, 0, :, :], b_nat[:, 1, :, :], z(2), ALU.mult))
                pstep(dve.tensor_tensor(b_tmp[:, 1, :, :], b_nat[:, 0, :, :], z(3), ALU.mult))
                pstep(dve.tensor_tensor(bb[:, 1, :, :], b_tmp[:, 0, :, :], b_tmp[:, 1, :, :], ALU.add))
                assert step[0] == 32

                def turns(i, jj):
                    b, tile = jj % 2, 4 * i + jj
                    dve.tensor_scalar(fr[:, b, :], steps[:, :], pc[:, 0, jj:jj + 1], None, ALU.mult).then_inc(fr_step, 1)
                    dve.wait_ge(fr_step, 2 * tile + 1)
                    dve.tensor_scalar(kk[:, b, :], fr[:, b, :], MAGIC, -MAGIC, ALU.add, ALU.add).then_inc(fr_step, 1)
                    dve.wait_ge(fr_step, 2 * tile + 2)
                    dve.tensor_tensor(fr[:, b, :], fr[:, b, :], kk[:, b, :], ALU.subtract).then_inc(fr_ready, 1)

                def scan(i, jj):
                    b, tile = jj % 2, 4 * i + jj
                    bu = ps[:, b, :].rearrange("p (a n) -> p a n", a=2)
                    dve.wait_ge(bu_ready, tile + 1)
                    dve.wait_ge(tab_ready, tile + 1)
                    dve.tensor_tensor(t1[:, :, :], bu, cs[:, b:b + 1, :].broadcast_to([P, 2, SEQ]), ALU.mult)
                    dve.tensor_tensor(t2[:, :, :], bu[:, ::-1, :], sn[:, b, :, :], ALU.mult).then_inc(rot_step, 1)
                    dve.wait_ge(rot_step, 2 * tile + 1)
                    if not (isinstance(tile, int) and tile == 0):
                        dve.wait_ge(g_ready, tile)
                    dve.tensor_tensor(vv[:, :, :], t1[:, :, :], t2[:, :, :], ALU.add).then_inc(rot_step, 1)
                    dve.wait_ge(rot_step, 2 * tile + 2)
                    if not (isinstance(tile, int) and tile == 0):
                        dve.wait_ge(pool_step, tile)
                    for r in range(2):
                        ins = dve.tensor_tensor_scan(gg[:, r, :], pc[:, 1, jj:jj + 1].broadcast_to([P, SEQ]), vv[:, r, :],
                                                     0.0, ALU.mult, ALU.add)
                    ins.then_inc(g_ready, 1)

                def y_out(i):
                    dve.wait_ge(y_mm, 4 * i + 4)
                    u = tile_ap(proj, i, SEQ_COLS)
                    d = vecs[:, V_D + i:V_D + i + 1] if isinstance(i, int) else vecs[:, bass.ds(V_D + i, 1)]
                    dve.scalar_tensor_tensor(out=u, in0=u, scalar=d, in1=ps[:, 4, 0:SEQ], op0=ALU.mult, op1=ALU.add).then_inc(y_ready, 1)

                def body(i):
                    four = bass.ds(4 * i, 4) if not isinstance(i, int) else slice(4 * i, 4 * i + 4)
                    if not (isinstance(i, int) and i == 0):
                        dve.wait_ge(g_ready, 4 * i)
                    dve.tensor_copy(pc[:, :, :], par[:, 0:2, four])
                    dve.tensor_copy(ui[:, :], tile_ap(proj, i, SEQ_COLS)).then_inc(ui_ready, 1)
                    dve.wait_ge(ui_ready, i + 1)
                    turns(i, 0)
                    turns(i, 1)
                    for jj in range(4):
                        scan(i, jj)
                        if jj < 2:
                            turns(i, jj + 2)
                        if jj == 1 and not (isinstance(i, int) and i == 0):
                            y_out(i - 1)

                body(0)
                loop(dve, 1, 8, body)
                y_out(7)
                dve.wait_ge(ada_done, 96)
                link(dve, "dve", dve.tensor_tensor(mod[:, 32:96], ps[:, 7, 32:96], bada[:, 32:96], ALU.add))
                link(dve, "dve", dve.tensor_scalar(gain[:, :], mod[:, 64:80], 1.0, None, ALU.add))
                link(dve, "dve", dve.tensor_tensor(gain[:, :], gain[:, :], vecs[:, V_N2:V_N2 + 16], ALU.mult))

            @block.tensor
            def _(pe):
                ada = byname["ada2"]
                pe.wait_ge(pre_dve, 26)
                for n, s_ in enumerate((7, 3, 14, 15)):
                    mm = pe.transpose(ps[:, 5, 32 * n:32 * n + 32], pre[:, s_, :], ident[0:32, 0:32])
                mm.then_inc(par_t, 1)

                def drive(i, jj):
                    b, tile = jj % 2, 4 * i + jj
                    if not (isinstance(tile, int) and tile < 2):
                        pe.wait_ge(rot_step, 2 * (tile - 2) + 1)
                    rows_ = slice(32 * jj, 32 * jj + 32)
                    for r in range(2):
                        mm = pe.matmul(ps[:, b, SEQ * r:SEQ * r + SEQ], bt[rows_, r, :], ui[rows_, :],
                                       start=True, stop=True)
                    mm.then_inc(bu_ready, 1)

                def read_out(i, jj):
                    b, tile = jj % 2, 4 * i + jj
                    pe.wait_ge(h_ready, tile + 1)
                    for r in range(2):
                        mm = pe.matmul(ps[:, 4, 0:SEQ], ct[:, r, P * jj:P * jj + P], hh[:, b, r, :],
                                       start=(jj == 0 and r == 0), stop=(jj == 3 and r == 1))
                    mm.then_inc(y_mm, 1)

                def body(i):
                    pe.wait_ge(e_ready, i + 1)
                    for r in range(2):
                        mm = pe.transpose(ps[:, 2, P * r:P * r + P], ebuf[:, r, :, :].rearrange("p j c -> p (j c)"), ident)
                    mm.then_inc(bt_ps, 1)
                    for r in range(2):
                        mm = pe.transpose(ps[:, 3, P * r:P * r + P], cd[:, r, :, :].rearrange("p d n -> p (d n)"), ident)
                    mm.then_inc(ct_ps, 1)
                    pe.wait_ge(bt_ready, i + 1)
                    pe.wait_ge(ui_ready, i + 1)
                    drive(i, 0)
                    drive(i, 1)
                    pe.wait_ge(ct_ready, i + 1)
                    if not (isinstance(i, int) and i == 0):
                        pe.wait_ge(y_ready, i)
                    for jj in range(4):
                        for n in range(2):
                            j = 2 * jj + n
                            ada_chunk(pe, ada, i, j, 8 + 2 * i + j // 4, 7)
                        read_out(i, jj)
                        if jj < 2:
                            drive(i, jj + 2)

                body(0)
                loop(pe, 1, 8, body)

        def span(b, qt):
            return slice(META if b == 0 else 0, META + P * (qt + 1))

        def head_cols(b):
            return SEQ_COLS if b == 0 else slice(0, T)

        UNITS = [(h, qt) for h in range(HEADS) for qt in range(2)]

        def heads_act(act, b):
            cols = head_cols(b)
            n = cols.stop - cols.start
            for w in range(2):
                for h in range(HEADS):
                    t = 16 * b + 8 * w + h
                    if t >= 2:
                        act.wait_ge(hs_mm, t - 1)
                    act.activation(sq[:, t % 2, 0:n], proj[:, 8 + 8 * w + h, cols], ACT.Square).then_inc(hs_sq, 1)
                act.wait_ge(hs_ms, 2 * b + w + 1)
                act.activation(rq[:, 1, 0:n], rq[:, 0, 0:n], ACT.Sqrt).then_inc(hs_root, 1)

        def heads_pe(pe, b):
            cols = head_cols(b)
            n = cols.stop - cols.start
            for w in range(2):
                for h in range(HEADS):
                    t = 16 * b + 8 * w + h
                    pe.wait_ge(hs_sq, t + 1)
                    pe.matmul(ps[0:HEADS, w, 0:n], onehot(h), sq[:, t % 2, 0:n], start=(h == 0), stop=(h == HEADS - 1)).then_inc(hs_mm, 1)
            for w in range(2):
                pe.wait_ge(hs_rstd, 2 * b + w + 1)
                for h in range(HEADS):
                    t = 16 * b + 8 * w + h
                    if t >= 2:
                        pe.wait_ge(hs_done, t - 1)
                    pe.matmul(ps[:, 2 + t % 2, 0:n], sel[:, h, :], rq[:, 3 + w, 0:n], start=True, stop=True).then_inc(hs_bc, 1)

        def heads_dve(dve, b):
            cols = head_cols(b)
            n = cols.stop - cols.start
            for w in range(2):
                dve.wait_ge(hs_mm, 16 * b + 8 * w + 8)
                if w:
                    dve.wait_ge(hs_root, 2 * b + 1)
                dve.tensor_scalar(rq[:, 0, 0:n], ps[0:HEADS, w, 0:n], 1.0 / P, EPS, ALU.mult, ALU.add).then_inc(hs_ms, 1)
                dve.wait_ge(hs_root, 2 * b + w + 1)
                link(dve, "dve", dve.reciprocal(rq[:, 1, 0:n], rq[:, 1, 0:n]))
                link(dve, "dve", dve.tensor_tensor(rq[:, 2, 0:n], rq[:, 1, 0:n], rq[:, 1, 0:n], ALU.mult))
                link(dve, "dve", dve.tensor_tensor(rq[:, 2, 0:n], rq[:, 2, 0:n], rq[:, 0, 0:n], ALU.mult))
                link(dve, "dve", dve.tensor_scalar(rq[:, 2, 0:n], rq[:, 2, 0:n], -0.5, 1.5, ALU.mult, ALU.add))
                dve.tensor_tensor(rq[:, 3 + w, 0:n], rq[:, 1, 0:n], rq[:, 2, 0:n], ALU.mult).then_inc(hs_rstd, 1)
                dve.wait_ge(hs_rstd, 2 * b + w + 1)
            for w in range(2):
                for h in range(HEADS):
                    t = 16 * b + 8 * w + h
                    x = proj[:, 8 + 8 * w + h, cols]
                    dve.wait_ge(hs_bc, t + 1)
                    dve.scalar_tensor_tensor(out=x, in0=x, scalar=qk_gain[:, 2 * b + w:2 * b + w + 1], in1=ps[:, 2 + t % 2, 0:n],
                                             op0=ALU.mult, op1=ALU.mult).then_inc(hs_done, 1)

        VG = [4, 6]

        def v_groups(b):
            return [(4 * b + i, i // 2, 4 * (i % 2)) for i in range(VG[b])]

        def v_pe(pe, b):
            for g, kt, h0 in v_groups(b):
                if g >= 2:
                    pe.wait_ge(v_copied, g - 1)
                for h in range(h0, h0 + 4):
                    c = 128 * (h - h0)
                    if kt < 2:
                        mm = pe.transpose(ps[:, 4 + g % 2, c:c + P], proj[:, 24 + h, META + P * kt:META + P * kt + P], ident)
                    else:
                        mm = pe.transpose(ps[0:META, 4 + g % 2, c:c + P], proj[:, 24 + h, 0:META], ident)
                mm.then_inc(v_t, 1)

        def v_act(act, b):
            for g, kt, h0 in v_groups(b):
                act.wait_ge(v_t, g + 1)
                r = P if kt < 2 else META
                act.activation(vt[0:r, kt, h0:h0 + 4, :], ps[0:r, 4 + g % 2, :].rearrange("p (h n) -> p h n", h=4),
                               ACT.Copy).then_inc(v_copied, 1)

        def key_tiles(b, qt):
            first = 0 if b == 0 else META
            tiles = [(slice(first + P * k, first + P * k + P), P, k) for k in range(qt + 1)]
            return tiles + ([(slice(0, META), META, 2)] if b else [])

        def units_pe(pe, b):
            def scores(i):
                h, qt = UNITS[i]
                u = 16 * b + i
                keys = span(b, qt)
                n = keys.stop - keys.start
                if u >= 2:
                    pe.wait_ge(logit, u - 1)
                qs = slice(META + P * qt, META + P * qt + P)
                mm = pe.matmul(ps[:, u % 2, 0:n], proj[:, 8 + h, qs], proj[:, 16 + h, keys], start=True, stop=(b == 0))
                if b:
                    mm = pe.matmul(ps[:, u % 2, 0:n], sel[:, h, :], fg[:, 3, keys], start=False, stop=True)
                mm.then_inc(score, 1)

            def turn(i):
                h, qt = UNITS[i]
                u = 16 * b + i
                pe.wait_ge(p_norm, u + 1)
                if u >= 2:
                    pe.wait_ge(p_copied, u - 1)
                for cols, r, k in key_tiles(b, qt):
                    mm = pe.transpose(ps[0:r, 2 + u % 2, P * k:P * k + P], pn[:, u % 2, cols], ident)
                mm.then_inc(p_t, 1)

            def weigh(i):
                h, qt = UNITS[i]
                u = 16 * b + i
                pe.wait_ge(p_copied, u + 1)
                if u >= 2:
                    pe.wait_ge(pv_free, u - 1)
                tiles = key_tiles(b, qt)
                for n, (cols, r, k) in enumerate(tiles):
                    mm = pe.matmul(ps[:, 6 + u % 2, 0:P], vt[0:r, k, h, :], pt[0:r, u % 2, P * k:P * k + P],
                                   start=(n == 0), stop=(n == len(tiles) - 1))
                mm.then_inc(pv, 1)

            pe.wait_ge(hs_done, 16 * (b + 1))
            for s_ in range(len(UNITS) + 2):
                if s_ < len(UNITS):
                    scores(s_)
                if 1 <= s_ <= len(UNITS):
                    turn(s_ - 1)
                if s_ == 2:
                    pe.wait_ge(v_copied, sum(VG[:b + 1]))
                    if b:
                        pe.wait_ge(pm_free, HEADS)
                if s_ >= 2:
                    weigh(s_ - 2)

        def units_act(act, b):
            for s_ in range(len(UNITS) + 2):
                if s_ < len(UNITS):
                    i = s_
                    h, qt = UNITS[i]
                    u = 16 * b + i
                    n = span(b, qt).stop - span(b, qt).start
                    act.wait_ge(negmax, u + 1)
                    if u >= 2:
                        act.wait_ge(p_norm, u - 1)
                    if b:
                        act.activation(ex[:, u % 2, 0:n], lg[:, u % 2, 0:n], ACT.Exp, bias=st[:, u % 2, 1:2],
                                       accum_out=st[:, u % 2, 2:3]).then_inc(expd, 1)
                    else:
                        act.activation(ex[:, u % 2, 0:n], lg[:, u % 2, 0:n], ACT.Exp, bias=st[:, u % 2, 1:2]).then_inc(expd, 1)
                if 1 <= s_ <= len(UNITS):
                    i = s_ - 1
                    h, qt = UNITS[i]
                    u = 16 * b + i
                    act.wait_ge(p_t, u + 1)
                    if u >= 2:
                        act.wait_ge(pv, u - 1)
                    w = P * (qt + 1)
                    ins = act.activation(pt[:, u % 2, 0:w], ps[:, 2 + u % 2, 0:w], ACT.Copy)
                    if b:
                        ins = act.activation(pt[0:META, u % 2, 2 * P:3 * P], ps[0:META, 2 + u % 2, 2 * P:3 * P], ACT.Copy)
                    ins.then_inc(p_copied, 1)
                if s_ >= 2:
                    i = s_ - 2
                    h, qt = UNITS[i]
                    u = 16 * b + i
                    act.wait_ge(pv, u + 1)
                    act.activation(act_hi[:, 8 + h, META + P * qt:META + P * qt + P], ps[:, 6 + u % 2, 0:P], ACT.Copy).then_inc(pv_hi, 1)

        def units_dve(dve, b):
            for s_ in range(len(UNITS) + 2):
                if s_ < len(UNITS):
                    i = s_
                    h, qt = UNITS[i]
                    u = 16 * b + i
                    n = span(b, qt).stop - span(b, qt).start
                    x = lg[:, u % 2, 0:n]
                    dve.wait_ge(score, u + 1)
                    if b:
                        c0 = 0 if qt == 0 else META + P
                        dve.scalar_tensor_tensor(out=x, in0=ps[:, u % 2, 0:n], scalar=cq[:, qt, h:h + 1], in1=causal[:, c0:c0 + n],
                                                 op0=ALU.add, op1=ALU.add).then_inc(logit, 1)
                    else:
                        c0 = 0 if qt == 0 else P
                        dve.scalar_tensor_tensor(out=x, in0=dil[:, c0:c0 + n], scalar=-(2.0 ** -(h + 1)), in1=ps[:, u % 2, 0:n],
                                                 op0=ALU.mult, op1=ALU.add).then_inc(logit, 1)
                    dve.wait_ge(logit, u + 1)
                    link(dve, "dve", dve.tensor_reduce(st[:, u % 2, 0:1], x, AX_X, ALU.max))
                    dve.tensor_scalar(st[:, u % 2, 1:2], st[:, u % 2, 0:1], -1.0, None, ALU.mult).then_inc(negmax, 1)
                if 1 <= s_ <= len(UNITS):
                    i = s_ - 1
                    h, qt = UNITS[i]
                    u = 16 * b + i
                    n = span(b, qt).stop - span(b, qt).start
                    dve.wait_ge(expd, u + 1)
                    if u >= 2:
                        dve.wait_ge(p_t, u - 1)
                    e = ex[:, u % 2, 0:n]
                    if b == 0:
                        c0 = 3 * P if qt == 0 else 4 * P
                        link(dve, "dve", dve.scalar_tensor_tensor(out=e, in0=e, scalar=1.0, in1=dil[:, c0:c0 + n], op0=ALU.mult,
                                                                  op1=ALU.mult, accum_out=st[:, u % 2, 2:3]))
                    link(dve, "dve", dve.reciprocal(st[:, u % 2, 3:4], st[:, u % 2, 2:3]))
                    dve.tensor_scalar(pn[:, u % 2, 0:n], e, st[:, u % 2, 3:4], None, ALU.mult).then_inc(p_norm, 1)
                if s_ >= 2:
                    i = s_ - 2
                    h, qt = UNITS[i]
                    u = 16 * b + i
                    dve.wait_ge(pv_hi, u + 1)
                    o = slice(META + P * qt, META + P * qt + P)
                    dve.tensor_tensor(act_lo[:, 8 + h, o], ps[:, 6 + u % 2, 0:P], act_hi[:, 8 + h, o].bitcast(F32),
                                      ALU.subtract).then_inc(pv_free, 1)

        block = nc.Block()
        with block:
            @block.sync
            def _(sp):
                sp.dma_start(sel[:, :, :], a["sel"].rearrange("a (h p) -> a h p", h=HEADS)).then_inc(mix_in, 16)
                sp.dma_start(dil[:, :], a["dilated"]).then_inc(mix_in, 16)

            @block.scalar
            def _(act):
                heads_act(act, 0)
                v_act(act, 0)
                units_act(act, 0)

            @block.vector
            def _(dve):
                heads_dve(dve, 0)
                dve.wait_ge(mix_in, SSM_IN + 32)
                units_dve(dve, 0)

            @block.tensor
            def _(pe):
                pe.wait_ge(mix_in, SSM_IN + 32)
                heads_pe(pe, 0)
                v_pe(pe, 0)
                units_pe(pe, 0)

        y_lo = hid_hi[:, 8:16, :]

        def glu_act(act, p, it, g):
            group_done(act, p, it, g)
            if g:
                act.wait_ge(glu_mul, g)
            act.activation(sig[:, :, 0:SEQ], bank(g, SEQ_COLS), ACT.Sigmoid).then_inc(bank_free[g], 1)

        def glu_dve(dve, p, it, g):
            dve.wait_ge(bank_free[g], group_index(p, it, g) + 1)
            s_ = slice(4 * g, 4 * g + 4)
            if g:
                dve.wait_ge(act_ready, ACT0["mix1"] + g)
            dve.tensor_tensor(val[:, :, 0:SEQ], sig[:, :, 0:SEQ], proj[:, s_, SEQ_COLS], ALU.mult).then_inc(glu_mul, 1)
            dve.wait_ge(glu_mul, g + 1)
            link(dve, "dve", dve.tensor_copy(act_hi[:, s_, SEQ_COLS], val[:, :, 0:SEQ]))
            dve.tensor_tensor(act_lo[:, s_, SEQ_COLS], val[:, :, 0:SEQ], act_hi[:, s_, SEQ_COLS].bitcast(F32),
                              ALU.subtract).then_inc(act_ready, 1)

        def then(*fs):
            def run():
                for f in fs:
                    if f:
                        f()
            return run

        block = nc.Block()
        with block:
            @block.sync
            def _(sp):
                stream(sp, "w_out")
                for f in ("ffn1", "ffn2"):
                    for i in range(len(PARTS)):
                        stream(sp, f"{f}.up{i}")
                        stream(sp, f"{f}.down{i}")
                stream(sp, "w_in_2")
                stream(sp, "w_out_2", rest=False)

            @block.scalar
            def _(act):
                pend = run_phase(act, "glu", split_hi, bind(act, glu_act), None)
                pend = run_phase(act, "w_out", split_hi, bind(act, squares_of(4)), pend)
                pend = ffn_act(act, "ffn1", then(pend, lambda: norm_act(act, "norm2", 48)), squares_of(8))
                pend = ffn_act(act, "ffn2", then(pend, lambda: norm_act(act, "ffn1_2")), squares_of(12))
                pend = run_phase(act, "w_in_2", split_hi, bind(act, copy_out), then(pend, lambda: norm_act(act, "mix_2")))
                pend()

            @block.vector
            def _(dve):
                dve.wait_ge(gelu_done, 2)
                link(dve, "dve", dve.tensor_copy(hid_hi[:, 0:8, SEQ_COLS], proj[:, 0:8, SEQ_COLS]))
                dve.tensor_tensor(hid_hi[:, 8:16, SEQ_COLS], proj[:, 0:8, SEQ_COLS], hid_hi[:, 0:8, SEQ_COLS].bitcast(F32),
                                  ALU.subtract).then_inc(y_split, 1)
                pend = run_phase(dve, "glu", split_lo, bind(dve, glu_dve), None)
                gate1 = with_squares(4, add_dve(("mod", 32)))
                pend = run_phase(dve, "w_out", split_lo, bind(dve, gate1), pend)
                pend = ffn_dve(dve, "ffn1", then(pend, lambda: norm_dve(dve, "norm2", gain, 0, 48)), add_dve(("mod", 80)),
                               with_squares(8, add_dve(("mod", 80))))
                pend = ffn_dve(dve, "ffn2", then(pend, lambda: norm_dve(dve, "ffn1_2", vecs, V_F1)), add_dve(("const", 0.5)),
                               with_squares(12, add_dve(("const", 0.5))))
                pend = run_phase(dve, "w_in_2", split_lo, nothing, then(pend, lambda: norm_dve(dve, "mix_2", vecs, V_MIX)))

            @block.tensor
            def _(pe):
                products(pe, "glu", hid_hi, y_lo, SEQ_COLS, lambda c: (y_split, 1))
                products(pe, "w_out", act_hi, act_lo, SEQ_COLS, lambda c: (act_ready, ACT0["mix1"] + c + 1) if c < 2 else None)
                norm_pe(pe, "norm2")
                ffn_pe(pe, "ffn1", ACT0["norm2"])
                norm_pe(pe, "ffn1_2")
                ffn_pe(pe, "ffn2", ACT0["ffn1_2"])
                norm_pe(pe, "mix_2")
                products(pe, "w_in_2", act_hi, act_lo, slice(0, T), counted(act_ready, ACT0["mix_2"]))

        block = nc.Block()
        with block:
            MIX2 = SSM_IN + 16 * 7

            @block.sync
            def _(sp):
                sp.dma_start(sel[:, :, :], a["sel"].rearrange("a (h p) -> a h p", h=HEADS)).then_inc(mix_in, 16)
                sp.dma_start(causal[:, :], a["causal"]).then_inc(mix_in, 16)
                sp.dma_start(wf[:, :, :], a["w_in_2"][0][:, 4 * HALFW:4 * HALFW + HEADS].rearrange("(t p) n -> p t n", p=P)).then_inc(mix_in, 16)
                sp.dma_start(bf[:, :], a["b_forget_2"].rearrange("a h -> h a")).then_inc(mix_in, 16)
                sp.dma_start(pw[:, :, :, :], a["pool_w_2"][0].rearrange("g (k p) n -> p g k n", p=P)).then_inc(mix_in, 16)

            @block.gpsimd
            def _(pool):
                for g in range(4):
                    if g:
                        pool.wait_ge(pooled, g)
                    src = proj[:, 2 * g:2 * g + 2, :]
                    for l in range(g + 1):
                        w = 2 ** (l + 1)
                        dst = win[:, l % 2, :, :]
                        link(pool, "pool", pool.tensor_tensor(dst[:, :, w - 1:T], src[:, :, w - 1:T], src[:, :, w // 2 - 1:T - w // 2], ALU.add))
                        src = dst

            @block.scalar
            def _(act):
                heads_act(act, 1)
                v_act(act, 1)
                act.wait_ge(fg_step, 1)
                act.activation(fg[:, 1, :], fg[:, 0, :], ACT.Abs).then_inc(act_link, 1)
                act.wait_ge(act_link, 1)
                act.activation(fg[:, 1, :], fg[:, 1, :], ACT.Exp, scale=-1.0).then_inc(act_link, 1)
                act.wait_ge(act_link, 2)
                act.activation(fg[:, 1, :], fg[:, 1, :], ACT.Ln, bias=1.0).then_inc(act_link, 1)
                act.wait_ge(cq_t, 1)
                act.activation(cq[:, :, :], ps[:, 5, 0:2 * HEADS].rearrange("p (t h) -> p t h", t=2), ACT.Copy).then_inc(cq_ready, 1)
                for o in range(HEADS):
                    act.wait_ge(pmm, o + 1)
                    if o:
                        act.wait_ge(pm_free, o)
                    act.activation(pmix[:, :], ps[:, 6 + o % 2, 0:SEQ], ACT.Copy, scale=vecs[:, V_PS + o:V_PS + o + 1]).then_inc(pm_val, 1)
                units_act(act, 1)

            @block.vector
            def _(dve):
                heads_dve(dve, 1)
                dve.wait_ge(fg_mm, 1)
                dve.tensor_scalar(fg[:, 0, :], ps[0:HEADS, 4, 0:T], bf[:, 0:1], None, ALU.add).then_inc(fg_step, 1)
                dve.wait_ge(act_link, 3)
                link(dve, "dve", dve.scalar_tensor_tensor(out=fg[:, 0, :], in0=fg[:, 0, :], scalar=0.0, in1=fg[:, 1, :], op0=ALU.min, op1=ALU.subtract))
                dve.tensor_tensor_scan(fg[:, 2, :], ones[0:HEADS, 0:1].broadcast_to([HEADS, T]), fg[:, 0, :], 0.0, ALU.mult, ALU.add).then_inc(fg_step, 1)
                dve.wait_ge(fg_step, 2)
                dve.tensor_scalar(fg[:, 3, :], fg[:, 2, :], -1.0, None, ALU.mult).then_inc(fg_step, 1)
                done = 0
                for g in range(4):
                    done += g + 1
                    dve.wait_ge(pool_link, done)
                    x = proj[:, 2 * g:2 * g + 2, SEQ_COLS]
                    dve.scalar_tensor_tensor(out=x, in0=win[:, g % 2, :, SEQ_COLS], scalar=1.0 / 2 ** (g + 1), in1=x,
                                             op0=ALU.mult, op1=ALU.subtract).then_inc(pooled, 1)
                for o in range(HEADS):
                    dve.wait_ge(pm_val, o + 1)
                    link(dve, "dve", dve.tensor_copy(act_hi[:, o, SEQ_COLS], pmix[:, :]))
                    dve.tensor_tensor(act_lo[:, o, SEQ_COLS], pmix[:, :], act_hi[:, o, SEQ_COLS].bitcast(F32), ALU.subtract).then_inc(pm_free, 1)
                dve.wait_ge(mix_in, MIX2)
                dve.wait_ge(cq_ready, 1)
                units_dve(dve, 1)

            @block.tensor
            def _(pe):
                pe.wait_ge(mix_in, MIX2)
                for k in range(KT):
                    for x in (act_hi, act_lo):
                        mm = pe.matmul(ps[0:HEADS, 4, 0:T], wf[:, k, :], x[:, k, :].bitcast(F32),
                                       start=(k == 0 and x is act_hi), stop=(k == KT - 1 and x is act_lo))
                mm.then_inc(fg_mm, 1)
                heads_pe(pe, 1)
                pe.wait_ge(fg_step, 1)
                v_pe(pe, 1)
                pe.wait_ge(fg_step, 2)
                pe.wait_ge(v_copied, sum(VG))
                for qt in range(2):
                    mm = pe.transpose(ps[:, 5, HEADS * qt:HEADS * qt + HEADS], fg[:, 2, META + P * qt:META + P * qt + P], ident[0:HEADS, 0:HEADS])
                mm.then_inc(cq_t, 1)
                for o in range(HEADS):
                    g, m = divmod(o, 2)
                    pe.wait_ge(pooled, g + 1)
                    if o >= 2:
                        pe.wait_ge(pm_val, o - 1)
                    for k in range(2):
                        mm = pe.matmul(ps[:, 6 + o % 2, 0:SEQ], pw[:, g, k, P * m:P * m + P], proj[:, 2 * g + k, SEQ_COLS],
                                       start=(k == 0), stop=(k == 1))
                    mm.then_inc(pmm, 1)
                pe.wait_ge(fg_step, 3)
                units_pe(pe, 1)

        block = nc.Block()
        with block:
            @block.sync
            def _(sp):
                stream(sp, "w_out_2", head=False)
                for i in range(len(PARTS)):
                    stream(sp, f"ffn3.up{i}")
                    stream(sp, f"ffn3.down{i}")
                for n in range(8):
                    h, g = divmod(n, 4)
                    sp.wait_ge(out_copied, n + 1)
                    sp.dma_start(out[0, P * h:P * h + P, GROUP * g:GROUP * g + GROUP], outb[:, h, GROUP * g:GROUP * g + GROUP]).then_inc(out_done, 16)
                sp.wait_ge(out_done, 16 * 8)

            @block.scalar
            def _(act):
                pend = run_phase(act, "w_out_2", split_hi, bind(act, squares_of(16)), None)
                pend = ffn_act(act, "ffn3", then(pend, lambda: norm_act(act, "ffn2_2")), nothing)
                pend()
                for n in range(8):
                    h, g = divmod(n, 4)
                    act.wait_ge(out_t, n + 1)
                    act.activation(outb[:, h, GROUP * g:GROUP * g + GROUP], ps[:, n, :], ACT.Copy).then_inc(out_copied, 1)

            @block.vector
            def _(dve):
                pend = run_phase(dve, "w_out_2", split_lo, bind(dve, with_squares(16, add_dve(("const", 1.0)))), None)
                pend = ffn_dve(dve, "ffn3", then(pend, lambda: norm_dve(dve, "ffn2_2", vecs, V_F2)), add_dve(("const", 0.5)), add_dve(("const", 0.5)))
                pend()

            @block.tensor
            def _(pe):
                products(pe, "w_out_2", act_hi, act_lo, SEQ_COLS, lambda c: None)
                norm_pe(pe, "ffn2_2")
                ffn_pe(pe, "ffn3", ACT0["ffn2_2"])
                last = byname["ffn3.down2"]
                for half in range(2):
                    pe.wait_ge(bank_free[half], 1 + last.g1 // 2)
                for n in range(8):
                    h, g = divmod(n, 4)
                    for m in range(4):
                        mm = pe.transpose(ps[:, n, P * m:P * m + P], res[:, 4 * g + m, META + P * h:META + P * h + P], ident)
                    mm.then_inc(out_t, 1)


INPUTS = [
    "x", "c", "w_ada", "b_ada", "norm1_w", "w_in", "ssm_a_re", "ssm_a_im", "ssm_log_dt", "ssm_b_re", "ssm_b_im",
    "ssm_c_re", "ssm_c_im", "ssm_d", "ssm_w_glu", "q_norm_w", "k_norm_w", "w_out", "norm2_w", "w_ffn_gate",
    "w_ffn_up", "w_ffn_down", "meta_tokens_2", "ffn1_norm_2", "ffn1_w_gate_2", "ffn1_w_up_2", "ffn1_w_down_2",
    "mix_norm_2", "w_in_2", "b_forget_2", "q_norm_2", "k_norm_2", "pool_w_2", "pool_scale_2", "w_out_2",
    "ffn2_norm_2", "ffn2_w_gate_2", "ffn2_w_up_2", "ffn2_w_down_2",
]


def kernel(**inputs):
    import concourse.bacc as bacc
    from concourse.bass_utils import run_bass_kernel_spmd

    nc = bacc.Bacc("TRN2", target_bir_lowering=False, num_devices=1)
    arrays = {n: np.ascontiguousarray(inputs[n]) for n in INPUTS}
    arrays.update(constants())
    aps = {n: nc.dram_tensor(f"in_{n}", v.shape, mybir.dt.from_np(v.dtype), kind="ExternalInput").ap() for n, v in arrays.items()}
    out = nc.dram_tensor("out_x", (1, SEQ, D), F32, kind="ExternalOutput").ap()
    build(nc, aps, out)
    run = run_bass_kernel_spmd(nc, [{f"in_{n}": v for n, v in arrays.items()}], core_ids=[0])
    return run.results[0]["out_x"]
```

```python
from contextlib import ExitStack

import numpy as np

import concourse.bass as bass
from concourse import mybir

F32 = mybir.dt.float32
F32R = mybir.dt.float32r
ALU = mybir.AluOpType
ACT = mybir.ActivationFunctionType
AX_X = mybir.AxisListType.X

P = 128
D = 2048
KT = D // P
QUADS = KT // 4
SEQ = 256
META = 16
T = META + SEQ
HALFW = D // 2
HEADS = HALFW // P
FF = 5632
GROUP = 512
CK = 4
RING = 4
PARTS = (4, 4, 3)
STATES = 64
SSM_TILES = 64 * STATES // P
EPS = 1e-6
MAGIC = 1.5 * 2.0 ** 23
TWO_PI = 6.2831850
HALF_PI = float(np.float32(np.pi / 2))
PI_A = 6.28125
PI_B = 0.00193500518798828125
PI_C = float(2 * np.pi - 6.28125 - 0.00193500518798828125)
SEQ_COLS = slice(META, T)

V_C, V_N1, V_N2, V_F1, V_MIX, V_F2, V_D, V_PS, V_QK = 0, 16, 32, 48, 64, 80, 96, 104, 112
V_ROWS = 116

SHIFT1, SCALE1, GATE1, SHIFT2, SCALE2, GATE2 = 0, 16, 32, 48, 64, 80

C_IDENT, C_ONES, C_ONEHOT, C_END = 0, 128, 256, 256 + HEADS * HEADS


def constants():
    ident = np.eye(P, dtype=np.float32)
    onehot = np.tile(np.eye(HEADS, dtype=np.float32).reshape(1, -1), (P, 1))
    const = np.concatenate([ident, np.ones((P, P), np.float32), onehot], axis=1)
    steps = np.tile(np.arange(SEQ, dtype=np.float32), (P, 1))
    sel = np.zeros((HEADS, HEADS, P), np.float32)
    for h in range(HEADS):
        sel[h, h] = 1.0
    dist, mult, mask = [], [], []
    for qt in range(2):
        q = np.arange(P * qt, P * qt + P)[:, None]
        k = np.arange(P * (qt + 1))[None]
        d = q - k
        m = ((d >= 0) & (d <= 128)).astype(np.float32)
        m += (d >= 0) & (d % 4 == 0) & (d <= 512)
        m += (d >= 0) & (d % 16 == 0) & (d <= 2048)
        mult.append(m)
        dist.append(np.where(m > 0, d, 1e36).astype(np.float32))
        k2 = np.arange(META + P * (qt + 1))[None]
        mask.append(np.where(q + META >= k2, 0.0, -1e30).astype(np.float32))
    return {
        "const": const, "steps": steps, "sel": sel.reshape(HEADS, HEADS * P),
        "dilated": np.concatenate(dist + mult, axis=1), "causal": np.concatenate(mask, axis=1),
    }


class Phase:

    def __init__(self, tally, name, iters, groups, cpg, order):
        self.name, self.iters, self.groups, self.cpg, self.order = name, iters, groups, cpg, order
        self.body = len(order)
        self.per = {k: order.count(k) for k in "SV"}
        self.n0 = tally["n"]
        self.before = {k: tally[k] for k in "SV"}
        self.g0 = tally["g"]
        tally["n"] += iters * self.body
        for k in "SV":
            tally[k] += iters * self.per[k]
        tally["g"] += iters * groups
        self.g1 = tally["g"]
        assert self.n0 % RING == 0 and self.body % RING == 0 and self.g0 % 2 == 0 and groups % 2 == 0
        assert self.per["S"] == groups * cpg

    def nth(self, it, j):
        k = self.order[j]
        return self.before[k] + self.order[:j].count(k) + it * self.per[k]


def plan():
    tally = {"n": 0, "g": 0, "S": 0, "V": 0}
    ph = []

    def add(name, iters, groups, cpg, order=None):
        ph.append(Phase(tally, name, iters, groups, cpg, order or "S" * (groups * cpg)))

    def ffn(name):
        for i, groups in enumerate(PARTS):
            add(f"{name}.up{i}", groups, 2, 4, "SSVSSVSSVSSV" if name == "ffn1" and i == 0 else None)
            if groups == 4:
                add(f"{name}.down{i}", 2, 2, 4)
            else:
                add(f"{name}.down{i}", 1, 4, groups)

    add("ada1", 8, 0, 4, "VVVV")
    add("w_in", 4, 2, 4, "SSVSSVSSVSSV")
    add("attn", 1, 0, 4, "V" * 16)
    add("glu", 1, 2, 2)
    add("w_out", 2, 2, 4, "VS" * 8)
    ffn("ffn1")
    ffn("ffn2")
    add("w_in_2", 4, 2, 4)
    add("w_out_2", 2, 2, 4)
    ffn("ffn3")
    return ph


def build(nc, a, out):
    phases = plan()
    byname = {p.name: p for p in phases}
    order = {p.name: i for i, p in enumerate(phases)}
    stack = ExitStack()
    with stack:
        base = nc.sbuf_base + (-nc.sbuf_base) % 64
        cursor = [base]
        slab_bytes = nc.sbuf_usable_end - base - 2048
        stack.enter_context(nc.sbuf_tensor("slab", [P, (slab_bytes // 4)], F32))

        def at(name, shape, dt=F32, offset=None):
            n = 4 * int(np.prod(shape[1:]))
            if offset is None:
                offset = cursor[0]
                cursor[0] += (n + 63) // 64 * 64
                assert cursor[0] <= base + slab_bytes, (name, cursor[0] - base, slab_bytes)
            return nc.alloc_sbuf_tensor_at(name, shape, dt, offset=offset)

        raw = [at(f"raw{i}", [P, CK, GROUP]) for i in range(RING)]
        w_hi = [at(f"w_hi{i}", [P, CK, GROUP], F32R) for i in range(2)]
        w_lo = [at(f"w_lo{i}", [P, CK, GROUP], F32R) for i in range(2)]
        res = at("res", [P, KT, T])
        act_at = cursor[0]
        act_hi = at("act_hi", [P, KT, T], F32R)
        act_lo = at("act_lo", [P, KT, T], F32R)
        hid_at = cursor[0]
        hid_hi = at("hid_hi", [P, KT, T], F32R)
        hid_lo = at("hid_lo", [P, KT, T], F32R)
        two_at = cursor[0]
        sig = at("sig", [P, 4, T])
        val = at("val", [P, 4, T])
        proj_at = cursor[0]
        proj = at("proj", [P, 32, T])
        ssq_at = cursor[0]
        ssq = at("ssq", [P, QUADS, T])
        rstd = at("rstd", [P, T])
        rtmp = at("rtmp", [P, T])
        const = at("const", [P, C_END])
        vecs = at("vecs", [P, V_ROWS])
        mod = at("mod", [P, 96])
        bada = at("bada", [P, 96])
        gain = at("gain", [P, KT])
        cond = at("cond", [P, KT])
        half_pi = at("half_pi", [P, 1])
        qk_gain = at("qk_gain", [P, 4])
        ident = const[:, C_IDENT:C_IDENT + P]
        ones = const[:, C_ONES:C_ONES + P]

        def onehot(h):
            return const[:, C_ONEHOT + HEADS * h:C_ONEHOT + HEADS * (h + 1)]

        xin = at("xin", [P, 2, D], offset=hid_at)
        metain = at("metain", [META, D], offset=hid_at + 16384)
        vin = at("vin", [V_ROWS, P], offset=hid_at + 24576)
        badain = at("badain", [96, P], offset=hid_at + 24576 + 512)
        outb = at("outb", [P, 2, D], offset=hid_at)
        acc1 = at("acc1", [P, 8, GROUP], offset=proj_at)
        accg1 = at("accg1", [P, 4, GROUP], offset=hid_at)
        accs2 = at("accs2", [P, 4, GROUP], offset=act_at + 17408)
        accg2 = at("accg2", [P, 4, GROUP], offset=proj_at)
        accb2 = at("accb2", [P, 4, GROUP], offset=proj_at + 9216)
        area = {"a": [hid_at + 8192, two_at + 8704], "b": [act_at, act_at + 34816]}

        def over(which, name, shape, dt=F32):
            n = (4 * int(np.prod(shape[1:])) + 63) // 64 * 64
            o = area[which][0]
            area[which][0] += n
            assert area[which][0] <= area[which][1], name
            return at(name, shape, dt, offset=o)

        bb = over("a", "bb", [P, 2, SSM_TILES, 16])
        c_nat = over("a", "c_nat", [P, 2, 8, STATES])
        cd = over("a", "cd", [P, 2, 2, STATES])
        ct = over("a", "ct", [P, 2, 2, 4 * 160])
        ebuf = over("a", "ebuf", [P, 2, 4, 32])
        bt = over("a", "bt", [P, 2, 2, P])
        par = over("a", "par", [P, 4, SSM_TILES])
        pc = over("a", "pc", [P, 2, 2, 4])
        steps = over("a", "steps", [P, SEQ])
        ui = over("a", "ui", [P, 2, SEQ])
        bnat_at = area["b"][0]
        fr = over("b", "fr", [P, 2, SEQ])
        kk = over("b", "kk", [P, 2, SEQ])
        cs = over("b", "cs", [P, 2, SEQ])
        sn = over("b", "sn", [P, 2, 2, SEQ])
        t1 = over("b", "t1", [P, 2, SEQ])
        t2 = over("b", "t2", [P, 2, SEQ])
        vv = over("b", "vv", [P, 2, SEQ])
        gg = over("a", "gg", [P, 2, 2, SEQ])
        o1 = over("b", "o1", [P, 2, SEQ])
        o2 = over("b", "o2", [P, 2, SEQ])
        hh = over("b", "hh", [P, 2, 2, SEQ])
        b_nat = at("b_nat", [P, 2, SSM_TILES, 16], offset=bnat_at)
        b_tmp = at("b_tmp", [P, 2, SSM_TILES, 16], offset=bnat_at + 4096)
        pre = at("pre", [32, 18, P], offset=bnat_at + 8192)
        ldt = at("ldt", [32, 4], offset=bnat_at + 8192 + 18 * 512)
        area["m"] = [hid_at, two_at + 8704]
        sel = over("m", "sel", [HEADS, HEADS, P])
        vt = over("m", "vt", [P, 3, HEADS, P])
        unit_at = area["m"][0]
        lg = over("m", "lg", [P, 2, T])
        ex = over("m", "ex", [P, 2, T])
        pn = over("m", "pn", [P, 2, T])
        pt = over("m", "pt", [P, 2, 3 * P])
        area["m"][0] += 256
        win = at("win", [P, 2, 2, T], offset=unit_at)
        rq = at("rq", [HEADS, 5, T], offset=ssq_at)
        st = over("m", "st", [P, 2, 4])
        pw_at = area["m"][0]
        pw = over("m", "pw", [P, 4, 2, 256])
        dil = at("dil", [P, 768], offset=pw_at)
        wf = over("m", "wf", [P, KT, HEADS])
        wf_hi = over("m", "wf_hi", [P, KT, HEADS], F32R)
        wf_lo = over("m", "wf_lo", [P, KT, HEADS], F32R)
        causal = over("m", "causal", [P, 416])
        fg = over("m", "fg", [HEADS, 4, T])
        bf = over("m", "bf", [HEADS, 1])
        cq = over("m", "cq", [P, 2, HEADS])
        sq = at("sq", [P, 2, T])
        pmix = at("pmix", [P, SEQ])

        ps = stack.enter_context(nc.psum_tensor("ps", [P, 8, 512], F32))

        def sem(name):
            return stack.enter_context(nc.semaphore(name))

        raw_landed = [sem(f"raw_landed{i}") for i in range(RING)]
        hi_ready, lo_ready = sem("hi_ready"), sem("lo_ready")
        chunk_done = sem("chunk_done")
        bank_free = [sem("bank_free_a"), sem("bank_free_b")]
        sig_ready, glu_mul, hid_step, hid_ready = sem("sig_ready"), sem("glu_mul"), sem("hid_step"), sem("hid_ready")
        act_ready = sem("act_ready")
        sq_ready, ssq_ready, ssq_sum = sem("sq_ready"), sem("ssq_ready"), sem("ssq_sum")
        ms_ready, root_ready, norm_val, norm_bias = sem("ms_ready"), sem("root_ready"), sem("norm_val"), sem("norm_bias")
        dve_link, act_link, pool_link = sem("dve_link"), sem("act_link"), sem("pool_link")
        const_in, vec_in, x_in, mix_in = sem("const_in"), sem("vec_in"), sem("x_in"), sem("mix_in")
        x_t, vec_t, vec_copied, cond_ready, mod_ready = sem("x_t"), sem("vec_t"), sem("vec_copied"), sem("cond_ready"), sem("mod_ready")
        res_in, acc_step, mod_sum, mod_read = (sem(n) for n in ("res_in", "acc_step", "mod_sum", "mod_read"))
        ssm_pre, par_t = sem("ssm_pre"), sem("par_t")
        ssm_tables, e_ready, bt_ps, bt_ready, ct_ps, ct_ready = (sem(n) for n in (
            "ssm_tables", "e_ready", "bt_ps", "bt_ready", "ct_ps", "ct_ready"))
        fr_step, fr_ready, tab_ready, bu_ready, rot_step, g_ready, pool_step, h_ready, y_mm, y_ready = (sem(n) for n in (
            "fr_step", "fr_ready", "tab_ready", "bu_ready", "rot_step", "g_ready", "pool_step", "h_ready", "y_mm", "y_ready"))
        pc_ready = sem("pc_ready")
        hs_sq, hs_mm, hs_ms, hs_root, hs_rstd, hs_bc, hs_done = (sem(n) for n in (
            "hs_sq", "hs_mm", "hs_ms", "hs_root", "hs_rstd", "hs_bc", "hs_done"))
        v_t, v_copied = sem("v_t"), sem("v_copied")
        score, logit, negmax, expd, wgt, p_norm, p_t, p_copied, pv, pv_hi, pv_free = (sem(n) for n in (
            "score", "logit", "negmax", "expd", "wgt", "p_norm", "p_t", "p_copied", "pv", "pv_hi", "pv_free"))
        ui_ready, tab_step, pre_act, pre_dve, e_free = (sem(n) for n in ("ui_ready", "tab_step", "pre_act", "pre_dve", "e_free"))
        gelu_done, y_split, pool_zero = sem("gelu_done"), sem("y_split"), sem("pool_zero")
        wf_split = sem("wf_split")
        fg_mm, fg_step, cq_t, cq_ready = sem("fg_mm"), sem("fg_step"), sem("cq_t"), sem("cq_ready")
        pooled, pmm, pm_val, pm_hi, pm_free = sem("pooled"), sem("pmm"), sem("pm_val"), sem("pm_hi"), sem("pm_free")
        out_t, out_copied, out_done = sem("out_t"), sem("out_copied"), sem("out_done")

        def rows(w, r0, r1):
            return w[r0:r1, :].rearrange("(t p) n -> p t n", p=P)

        ada_rows = rows(a["w_ada"][0], 0, D)

        def w_ada(c, col):
            return ada_rows[:, CK * c:CK * c + CK, bass.ds(col, GROUP)]

        def source(name):
            if name == "ada1":
                return lambda it, j: w_ada(j, it * GROUP)
            if name == "attn":
                return lambda it, j: w_ada(j % 4, SCALE2 * P + (j // 4) * GROUP)
            if name == "glu":
                w = rows(a["ssm_w_glu"][0], 0, HALFW)
                return lambda it, j: w[:, CK * (j % 2):CK * (j % 2) + CK, (j // 2) * GROUP:(j // 2) * GROUP + GROUP]
            if name in ("w_in", "w_out", "w_in_2", "w_out_2"):
                w = rows(a[name][0], 0, D)
                first, per = (GATE1, 1) if name == "w_in" else (SHIFT2, 2)
                return lambda it, j, v=None: w_ada(v % 4, first * P + (it * per + v // 4) * GROUP) if v is not None else w[:, CK * (j % 4):CK * (j % 4) + CK, bass.ds((j // 4) * GROUP + it * (2 * GROUP), GROUP)]
            ffn, what = name.split(".")
            names = {"ffn1": ("w_ffn_gate", "w_ffn_up", "w_ffn_down"), "ffn2": ("ffn1_w_gate_2", "ffn1_w_up_2", "ffn1_w_down_2"),
                     "ffn3": ("ffn2_w_gate_2", "ffn2_w_up_2", "ffn2_w_down_2")}[ffn]
            part = int(what[-1])
            h0 = GROUP * sum(PARTS[:part])
            if what.startswith("up"):
                wg, wu = rows(a[names[0]][0], 0, D), rows(a[names[1]][0], 0, D)
                return lambda it, j, v=None: w_ada(v, GATE2 * P + it * GROUP) if v is not None else (wg if j < 4 else wu)[:, CK * (j % 4):CK * (j % 4) + CK, bass.ds(h0 + it * GROUP, GROUP)]
            w = rows(a[names[2]][0], h0, h0 + GROUP * PARTS[part])
            cpg = byname[name].cpg
            per = byname[name].groups
            return lambda it, j: w[:, CK * (j % cpg):CK * (j % cpg) + CK, bass.ds((j // cpg) * GROUP + it * (per * GROUP), GROUP)]

        def loop(eng, start, end, body):
            if end - start == 1:
                body(start)
            elif end > start:
                with eng.Fori(start, end) as i:
                    body(i)

        def used(p, it, j):
            n = p.nth(it, j) + 1
            return {"S": (lo_ready, n), "V": (acc_step, CK * n)}[p.order[j]]

        def stream(sp, name, head=True, rest=True):
            p = byname[name]
            src = source(name)
            prev = phases[order[name] - 1] if order[name] else None

            mixed = p.per["S"] and p.per["V"]

            def body(it, first=False):
                for j in range(p.body):
                    if first and not (head if j < RING else rest):
                        continue
                    if j >= RING:
                        sp.wait_ge(*used(p, it, j - RING))
                    elif not first:
                        sp.wait_ge(*used(p, it - 1, p.body - RING + j))
                    elif prev is not None:
                        sp.wait_ge(*used(prev, prev.iters - 1, prev.body - RING + j))
                    kind = p.order[j]
                    if mixed:
                        at_ = p.order[:j].count(kind)
                        src_ = src(it, at_) if kind == "S" else src(it, 0, at_)
                    else:
                        src_ = src(it, j)
                    sp.dma_start(raw[j % RING][:, :, :], src_).then_inc(raw_landed[j % RING], 16)

            body(0, True)
            if rest:
                loop(sp, 1, p.iters, body)

        def landed(eng, p, it, j):
            eng.wait_ge(raw_landed[j % RING], 16 * (p.n0 // RING + j // RING + 1) + it * (16 * p.body // RING))

        def split_hi(act, p, it, j):
            b = p.order[:j].count("S") % 2
            landed(act, p, it, j)
            n = p.nth(it, j)
            if not (isinstance(n, int) and n < 2):
                act.wait_ge(chunk_done, n - 1)
            act.activation(w_hi[b][:, :, :], raw[j % RING][:, :, :], ACT.Copy).then_inc(hi_ready, 1)

        def split_lo(dve, p, it, j):
            b = p.order[:j].count("S") % 2
            dve.wait_ge(hi_ready, p.nth(it, j) + 1)
            dve.tensor_tensor(w_lo[b][:, :, :], raw[j % RING][:, :, :], w_hi[b][:, :, :].bitcast(F32),
                              ALU.subtract).then_inc(lo_ready, 1)

        def condition(dve, p, it, j, acc, c):
            landed(dve, p, it, j)
            v = p.nth(it, j)
            for t in range(CK):
                w, x = raw[j % RING][:, t, :], cond[:, CK * c + t:CK * c + t + 1]
                if not (isinstance(v, int) and v == 0 and t == 0):
                    dve.wait_ge(acc_step, CK * v + t)
                if c == 0 and t == 0:
                    dve.tensor_scalar(acc, w, x, None, ALU.mult).then_inc(acc_step, 1)
                else:
                    dve.scalar_tensor_tensor(out=acc, in0=w, scalar=x, in1=acc, op0=ALU.mult, op1=ALU.add).then_inc(acc_step, 1)

        def gather(pe, acc, bank_, col):
            for m in range(4):
                mm = pe.matmul(ps[:, bank_, col + m:col + m + 1], acc[:, P * m:P * m + P], ones[:, 0:1], start=True, stop=True,
                               skip_group_check=True)
            mm.then_inc(mod_sum, 1)

        def acc_of(buf, it):
            return buf[:, it, :] if isinstance(it, int) else buf[:, bass.ds(it, 1), :].rearrange("p a n -> p (a n)")

        def run_phase(eng, name, split, evac, pending, acc=None, norm=False):
            p = byname[name]

            def body(it, first=False):
                sj = 0
                for j in range(p.body):
                    if p.order[j] == "V":
                        if acc is not None:
                            v = p.order[:j].count("V")
                            condition(eng, p, it, j, acc_of(acc, it * (p.per["V"] // 4) + v // 4), v % 4)
                        continue
                    if first and norm and sj == 1:
                        pending(lambda: split(eng, p, it, j))
                        sj += 1
                        continue
                    split(eng, p, it, j)
                    if sj % p.cpg == 1:
                        g = sj // p.cpg
                        if g:
                            evac(p, it, g - 1)
                        elif first:
                            if pending:
                                pending()
                        else:
                            evac(p, it - 1, p.groups - 1)
                    sj += 1

            body(0, True)
            loop(eng, 1, p.iters, body)
            return lambda: evac(p, p.iters - 1, p.groups - 1)

        def group_done(eng, p, it, g):
            eng.wait_ge(chunk_done, p.before["S"] + it * p.per["S"] + (g + 1) * p.cpg)

        def group_index(p, it, g):
            return 1 + p.g0 // 2 + g // 2 + it * (p.groups // 2)

        def bank(half, cols):
            return ps[:, 4 * half:4 * half + 4, 0:cols.stop - cols.start]

        def counted(sem_, base_):
            return lambda c: (sem_, base_ + c + 1)

        def products(pe, name, hi, lo, cols, ready):
            p = byname[name]
            n = cols.stop - cols.start

            def body(it):
                for j in range(p.per["S"]):
                    g, c = divmod(j, p.cpg)
                    half = g % 2
                    if c == 0:
                        pe.wait_ge(bank_free[half], group_index(p, it, g))
                    if ready(c) is not None:
                        pe.wait_ge(*ready(c))
                    pe.wait_ge(lo_ready, p.before["S"] + it * p.per["S"] + j + 1)
                    for t in range(CK):
                        k = CK * c + t
                        for m in range(4):
                            o = ps[:, 4 * half + m, 0:n]
                            whi, wlo = w_hi[j % 2][:, t, P * m:P * m + P], w_lo[j % 2][:, t, P * m:P * m + P]
                            pe.matmul(o, whi, hi[:, k, cols], start=(k == 0), stop=False)
                            pe.matmul(o, whi, lo[:, k, cols], start=False, stop=False)
                            mm = pe.matmul(o, wlo, hi[:, k, cols], start=False, stop=(k == CK * p.cpg - 1))
                    mm.then_inc(chunk_done, 1)

            loop(pe, 0, p.iters, body)

        linked = {"dve": 0, "act": 0, "pool": 0}

        def link(eng, which, ins):
            s = {"dve": dve_link, "act": act_link, "pool": pool_link}[which]
            linked[which] += 1
            ins.then_inc(s, 1)
            eng.wait_ge(s, linked[which])

        NORMS = ["norm1", "norm2", "ffn1_2", "mix_2", "ffn2_2"]

        def norm_pe(pe, name):
            i = NORMS.index(name)
            for g in range(QUADS):
                pe.wait_ge(ssq_ready, QUADS * i + g + 1)
                mm = pe.matmul(ps[:, 0, 0:T], ones, ssq[:, g, :], start=(g == 0), stop=(g == QUADS - 1))
            mm.then_inc(ssq_sum, 1)

        def root_act(act, name):
            act.wait_ge(ms_ready, NORMS.index(name) + 1)
            act.activation(rstd[:, :], rtmp[:, :], ACT.Sqrt).then_inc(root_ready, 1)

        def norm_act(act, name, shift=None):
            i = NORMS.index(name)
            if name != "norm1":
                root_act(act, name)
            if shift is not None:
                n = {"norm1": 0, "norm2": 1}[name]
                for q in range(QUADS):
                    v = (val, sig)[q % 2]
                    act.wait_ge(norm_val, QUADS * i + q + 1)
                    for t in range(4):
                        ins = act.activation(v[:, t, :], v[:, t, :], ACT.Identity,
                                             bias=mod[:, shift + 4 * q + t:shift + 4 * q + t + 1])
                    ins.then_inc(norm_bias, 1)

        def root_dve(dve, name):
            i = NORMS.index(name)
            dve.wait_ge(ssq_sum, i + 1)
            dve.tensor_scalar(rtmp[:, :], ps[:, 0, 0:T], 1.0 / D, EPS, ALU.mult, ALU.add).then_inc(ms_ready, 1)
            dve.wait_ge(root_ready, i + 1)
            link(dve, "dve", dve.reciprocal(rstd[:, :], rstd[:, :]))

        def norm_dve(dve, name, weight, w0, shift, second):
            i = NORMS.index(name)
            if name != "norm1":
                root_dve(dve, name)

            def scaled(q):
                v = (val, sig)[q % 2]
                if q >= 2:
                    dve.wait_ge(act_ready, ACT0[name] + q - 1)
                for t in range(4):
                    k = 4 * q + t
                    ins = dve.scalar_tensor_tensor(out=v[:, t, :], in0=res[:, k, :], scalar=weight[:, w0 + k:w0 + k + 1],
                                                   in1=rstd[:, :], op0=ALU.mult, op1=ALU.mult)
                ins.then_inc(norm_val, 1)

            scaled(0)
            for q in range(QUADS):
                if q + 1 < QUADS:
                    scaled(q + 1)
                v = (val, sig)[q % 2]
                s = slice(4 * q, 4 * q + 4)
                dve.wait_ge(norm_val, QUADS * i + q + 1)
                if shift is not None:
                    dve.wait_ge(norm_bias, QUADS * {"norm1": 0, "norm2": 1}[name] + q + 1)
                link(dve, "dve", dve.tensor_copy(act_hi[:, s, :], v[:, :, :]))
                dve.tensor_tensor(act_lo[:, s, :], v[:, :, :], act_hi[:, s, :].bitcast(F32), ALU.subtract).then_inc(act_ready, 1)
                if q == 0:
                    second()

        ACT0 = {}
        total = 0
        for nm, k in (("norm1", 4), ("mix1", 2), ("norm2", 4), ("ffn1_2", 4), ("mix_2", 4), ("ffn2_2", 4)):
            ACT0[nm] = total
            total += k

        def squares_act(act, q, count, n):
            act.activation(sig[:, :, :], res[:, 4 * q:4 * q + 4, :] if isinstance(q, int) else
                           res[:, bass.ds(4 * q, 4), :], ACT.Square).then_inc(sq_ready, 1)

        def squares_dve(dve, q, count):
            dve.wait_ge(sq_ready, count + 1)
            o = ssq[:, q, :] if isinstance(q, int) else ssq[:, bass.ds(q, 1), :].rearrange("p a n -> p (a n)")
            dve.tensor_reduce(o, sig[:, :, :].rearrange("p t n -> p n t"), AX_X, ALU.add).then_inc(ssq_ready, 1)

        def copy_out(act, p, it, g):
            group_done(act, p, it, g)
            cols = SEQ_COLS if p.name == "w_in" else slice(0, T)
            dst = proj[:, 4 * g:4 * g + 4, cols] if isinstance(it, int) and it == 0 else \
                proj[:, bass.ds(it * (4 * p.groups) + 4 * g, 4), cols]
            act.activation(dst, bank(g % 2, cols), ACT.Copy).then_inc(bank_free[g % 2], 1)

        FFNS = ("ffn1", "ffn2", "ffn3")

        def hid0(p):
            f, what = p.name.split(".")
            return sum(PARTS) * FFNS.index(f) + sum(PARTS[:int(what[-1])])

        def ffn_cols(name):
            return slice(0, T) if name.startswith("ffn2") else SEQ_COLS

        def gate_act(act, p, it, g):
            if g == 0:
                cols = ffn_cols(p.name)
                q = hid0(p) + it
                group_done(act, p, it, 0)
                act.wait_ge(bank_free[1], group_index(p, it, 1))
                act.activation(sig[:, :, 0:cols.stop - cols.start], bank(0, cols), ACT.Silu).then_inc(bank_free[0], 1)

        def gate_dve(dve, p, it, g):
            if g == 1:
                cols = ffn_cols(p.name)
                n = cols.stop - cols.start
                q = hid0(p) + it
                group_done(dve, p, it, 1)
                dve.wait_ge(bank_free[0], group_index(p, it, 0) + 1)
                if not (isinstance(q, int) and q == 0):
                    dve.wait_ge(hid_ready, q)
                dve.tensor_tensor(val[:, :, 0:n], sig[:, :, 0:n], bank(1, cols), ALU.mult).then_inc(bank_free[1], 1)
                dve.wait_ge(bank_free[1], group_index(p, it, 1) + 1)
                hi = hid_hi[:, 0:4, cols] if isinstance(it, int) and it == 0 else hid_hi[:, bass.ds(4 * it, 4), cols]
                lo = hid_lo[:, 0:4, cols] if isinstance(it, int) and it == 0 else hid_lo[:, bass.ds(4 * it, 4), cols]
                dve.tensor_copy(hi, val[:, :, 0:n]).then_inc(hid_step, 1)
                dve.wait_ge(hid_step, q + 1)
                dve.tensor_tensor(lo, val[:, :, 0:n], hi.bitcast(F32), ALU.subtract).then_inc(hid_ready, 1)

        def tile_ap(buf, k, cols):
            return buf[:, k, cols] if isinstance(k, int) else buf[:, bass.ds(k, 1), cols].rearrange("p a n -> p (a n)")

        def add_dve(scale):
            def evac(dve, p, it, g):
                cols = ffn_cols(p.name) if p.name.startswith("ffn") else SEQ_COLS
                n = cols.stop - cols.start
                group_done(dve, p, it, g)
                for m in range(4):
                    k = 4 * g + m + it * (4 * p.groups)
                    r = tile_ap(res, k, cols)
                    s = scale[1] if scale[0] == "const" else (
                        mod[:, scale[1] + k:scale[1] + k + 1] if isinstance(k, int) else mod[:, bass.ds(scale[1] + k, 1)])
                    ins = dve.scalar_tensor_tensor(out=r, in0=ps[:, 4 * (g % 2) + m, 0:n], scalar=s, in1=r,
                                                   op0=ALU.mult, op1=ALU.add)
                ins.then_inc(bank_free[g % 2], 1)
            return evac

        def with_squares(count, evac):
            def both(dve, p, it, g):
                evac(dve, p, it, g)
                squares_dve(dve, g + it * p.groups, count + g + it * p.groups)
            return both

        def squares_of(count):
            def sq_act(act, p, it, g):
                act.wait_ge(bank_free[g % 2], group_index(p, it, g) + 1)
                q = g + it * p.groups
                if not (isinstance(q, int) and q == 0):
                    act.wait_ge(ssq_ready, count + q)
                squares_act(act, q, count, T)
            return sq_act

        def nothing(*_):
            pass

        def bind(eng, f):
            return lambda p, it, g: f(eng, p, it, g)

        def gate2_pe(pe):
            p = byname["ffn1.up0"]
            pe.wait_ge(bank_free[0], group_index(byname["ffn1.down0"], 0, 0))
            for g in range(4):
                pe.wait_ge(acc_step, CK * (p.before["V"] + 4 * g + 4))
                gather(pe, accg2[:, g, :], 0, 4 * g)
            pe.wait_ge(mod_read, 1)

        def gate2_dve(dve):
            dve.wait_ge(mod_sum, 24)
            dve.tensor_tensor(mod[:, GATE2:GATE2 + 16], ps[:, 0, 0:16], bada[:, GATE2:GATE2 + 16], ALU.add).then_inc(mod_read, 1)
            dve.wait_ge(mod_read, 1)

        def ffn_pe(pe, f, ready0):
            for i, groups in enumerate(PARTS):
                cols = ffn_cols(f)
                if f == "ffn1" and i == 0:
                    after_up = gate2_pe
                else:
                    after_up = None
                products(pe, f"{f}.up{i}", act_hi, act_lo, cols, counted(act_ready, ready0))
                if after_up:
                    after_up(pe)
                products(pe, f"{f}.down{i}", hid_hi, hid_lo, cols, counted(hid_ready, hid0(byname[f"{f}.up{i}"])))

        def ffn_act(act, f, pending, last):
            for i in range(len(PARTS)):
                pending = run_phase(act, f"{f}.up{i}", split_hi, bind(act, gate_act), pending)
                e = last if i == len(PARTS) - 1 else nothing
                pending = run_phase(act, f"{f}.down{i}", split_hi, bind(act, e), pending)
            return pending

        def ffn_dve(dve, f, pending, evac, last):
            for i in range(len(PARTS)):
                up = run_phase(dve, f"{f}.up{i}", split_lo, bind(dve, gate_dve), pending, accg2 if f == "ffn1" and i == 0 else None,
                               norm=i == 0)

                def settle(up=up, p=byname[f"{f}.down{i}"]):
                    up()
                    if p.name == "ffn1.down0":
                        gate2_dve(dve)
                    if p.g0:
                        for h in range(2):
                            dve.wait_ge(bank_free[h], p.g0 // 2)
                pending = run_phase(dve, f"{f}.down{i}", split_lo, bind(dve, last if i == len(PARTS) - 1 else evac), settle)
            return pending

        block = nc.Block()
        with block:
            @block.sync
            def _(sp):
                sp.dma_start(vin[V_C:V_C + 16, :], a["c"].rearrange("a (t p) -> (a t) p", p=P)).then_inc(vec_in, 16)
                for row, nm in ((V_N1, "norm1_w"), (V_N2, "norm2_w"), (V_F1, "ffn1_norm_2"), (V_MIX, "mix_norm_2"), (V_F2, "ffn2_norm_2")):
                    sp.dma_start(vin[row:row + 16, :], a[nm].rearrange("a (t p) -> (a t) p", p=P)).then_inc(vec_in, 16)
                sp.dma_start(vin[V_D:V_D + 8, :], a["ssm_d"][0].rearrange("(t g) c -> t (g c)", t=8)).then_inc(vec_in, 16)
                sp.dma_start(vin[V_PS:V_PS + 8, :], a["pool_scale_2"].rearrange("a (t p) -> (a t) p", p=P)).then_inc(vec_in, 16)
                for i, nm in enumerate(("q_norm_w", "k_norm_w", "q_norm_2", "k_norm_2")):
                    sp.dma_start(vin[V_QK + i:V_QK + i + 1, :], a[nm]).then_inc(vec_in, 16)
                sp.dma_start(badain[:, :], a["b_ada"].rearrange("a (t p) -> (a t) p", p=P)).then_inc(vec_in, 16)
                stream(sp, "ada1")
                stream(sp, "w_in")
                stream(sp, "attn", rest=False)
                sp.wait_ge(x_in, 32)

            @block.scalar
            def _(act):
                act.dma_start(const[:, :], a["const"]).then_inc(const_in, 16)
                act.dma_start(xin[:, :, :], a["x"][0].rearrange("(t p) n -> p t n", p=P)).then_inc(x_in, 16)
                act.dma_start(metain[:, :], a["meta_tokens_2"]).then_inc(x_in, 16)
                act.wait_ge(vec_t, 2)
                act.activation(vecs[:, :], ps[:, 7, 0:V_ROWS], ACT.Copy).then_inc(vec_copied, 1)
                act.wait_ge(vec_t, 2)
                act.activation(bada[:, :], ps[:, 7, P:P + 96], ACT.Copy).then_inc(vec_copied, 1)
                act.wait_ge(vec_copied, 1)
                act.activation(cond[:, :], vecs[:, V_C:V_C + 16], ACT.Silu).then_inc(cond_ready, 1)
                for q in range(QUADS):
                    act.wait_ge(x_t, q + 1)
                    b = 2 * (q % 2)
                    act.activation(res[:, 4 * q:4 * q + 4, SEQ_COLS],
                                   ps[:, b:b + 2, :].rearrange("p b (t n) -> p (b t) n", n=SEQ), ACT.Copy).then_inc(res_in, 1)
                act.wait_ge(x_t, QUADS + 1)
                act.activation(res[:, :, 0:META], ps[:, 6, 0:KT * META].rearrange("p (t n) -> p t n", n=META),
                               ACT.Copy).then_inc(res_in, 1)
                act.wait_ge(res_in, QUADS + 1)
                for q in range(QUADS):
                    if q:
                        act.wait_ge(ssq_ready, q)
                    squares_act(act, q, q, T)
                root_act(act, "norm1")
                flush = run_phase(act, "w_in", split_hi, bind(act, copy_out), lambda: norm_act(act, "norm1", 0))
                flush()

            @block.vector
            def _(dve):
                dve.memset(half_pi[:, :], HALF_PI)
                dve.wait_ge(cond_ready, 1)

                def ada_body(it):
                    for j in range(4):
                        condition(dve, byname["ada1"], it, j, acc_of(acc1, it), j)
                ada_body(0)
                ada_body(1)
                for q in range(QUADS):
                    squares_dve(dve, q, q)
                loop(dve, 2, 5, ada_body)
                root_dve(dve, "norm1")
                loop(dve, 5, 8, ada_body)
                dve.wait_ge(vec_copied, 2)
                scale = float(P) ** -0.5
                dve.tensor_scalar(qk_gain[:, 0:1], vecs[:, V_QK:V_QK + 1], scale, None, ALU.mult)
                dve.tensor_copy(qk_gain[:, 1:2], vecs[:, V_QK + 1:V_QK + 2])
                dve.tensor_scalar(qk_gain[:, 2:3], vecs[:, V_QK + 2:V_QK + 3], scale, None, ALU.mult)
                dve.tensor_copy(qk_gain[:, 3:4], vecs[:, V_QK + 3:V_QK + 4])
                dve.wait_ge(mod_sum, 8)
                dve.tensor_tensor(mod[:, 0:32], ps[:, 5, 0:32], bada[:, 0:32], ALU.add).then_inc(bank_free[1], 1)
                dve.wait_ge(bank_free[1], 1)
                dve.tensor_scalar(gain[:, :], mod[:, 16:32], 1.0, None, ALU.add).then_inc(bank_free[0], 1)
                dve.wait_ge(bank_free[0], 1)
                link(dve, "dve", dve.tensor_tensor(gain[:, :], gain[:, :], vecs[:, V_N1:V_N1 + 16], ALU.mult))
                run_phase(dve, "w_in", split_lo, nothing, lambda second: norm_dve(dve, "norm1", gain, 0, 0, second), accg1, norm=True)

            @block.tensor
            def _(pe):
                pe.wait_ge(const_in, 16)
                pe.wait_ge(vec_in, 16 * 13)
                pe.transpose(ps[:, 7, 0:V_ROWS], vin[:, :], ident[0:V_ROWS, 0:V_ROWS]).then_inc(vec_t, 1)
                pe.transpose(ps[:, 7, P:P + 96], badain[:, :], ident[0:96, 0:96]).then_inc(vec_t, 1)
                pe.wait_ge(x_in, 32)
                for q in range(QUADS):
                    if q >= 2:
                        pe.wait_ge(res_in, q - 1)
                    for t in range(4):
                        for h in range(2):
                            mm = pe.transpose(ps[:, 2 * (q % 2) + t // 2, (t % 2) * SEQ + P * h:(t % 2) * SEQ + P * h + P],
                                              xin[:, h, P * (4 * q + t):P * (4 * q + t) + P], ident)
                    mm.then_inc(x_t, 1)
                for t in range(KT):
                    mm = pe.transpose(ps[:, 6, META * t:META * t + META], metain[:, P * t:P * t + P], ident[0:META, 0:META])
                mm.then_inc(x_t, 1)
                for g in range(8):
                    pe.wait_ge(acc_step, 4 * CK * (g + 1))
                    gather(pe, acc1[:, g, :], 5, 4 * g)
                    if g == 3:
                        norm_pe(pe, "norm1")
                products(pe, "w_in", act_hi, act_lo, SEQ_COLS, counted(act_ready, ACT0["norm1"]))

        def head_cols(b):
            return SEQ_COLS if b == 0 else slice(0, T)

        UNITS = [(h, qt) for h in range(HEADS) for qt in range(2)]

        def sum_bank(b, w):
            return ps[0:HEADS, w, 0:T] if b else ps[0:HEADS, 7, SEQ * w:SEQ * w + SEQ]

        def heads_act(act, b, parts="sr"):
            cols = head_cols(b)
            n = cols.stop - cols.start
            for w in range(2):
                for h in range(HEADS) if "s" in parts else ():
                    t = 16 * b + 8 * w + h
                    if t >= 2:
                        act.wait_ge(hs_mm, t - 1)
                    act.activation(sq[:, t % 2, 0:n], proj[:, 8 + 8 * w + h, cols], ACT.Square).then_inc(hs_sq, 1)
                if "r" in parts:
                    act.wait_ge(hs_ms, 2 * b + w + 1)
                    act.activation(rq[:, 1, 0:n], rq[:, 0, 0:n], ACT.Sqrt).then_inc(hs_root, 1)

        def heads_pe(pe, b):
            cols = head_cols(b)
            n = cols.stop - cols.start
            for w in range(2):
                for h in range(HEADS):
                    t = 16 * b + 8 * w + h
                    pe.wait_ge(hs_sq, t + 1)
                    pe.matmul(sum_bank(b, w), onehot(h), sq[:, t % 2, 0:n], start=(h == 0), stop=(h == HEADS - 1)).then_inc(hs_mm, 1)

        def heads_dve(dve, b):
            cols = head_cols(b)
            n = cols.stop - cols.start
            for w in range(2):
                dve.wait_ge(hs_mm, 16 * b + (8 * w + 8 if b else 16))
                if w:
                    dve.wait_ge(hs_root, 2 * b + 1)
                dve.tensor_scalar(rq[:, 0, 0:n], sum_bank(b, w), 1.0 / P, EPS, ALU.mult, ALU.add).then_inc(hs_ms, 1)
                dve.wait_ge(hs_root, 2 * b + w + 1)
                link(dve, "dve", dve.reciprocal(rq[:, 1, 0:n], rq[:, 1, 0:n]))
                link(dve, "dve", dve.tensor_tensor(rq[:, 2, 0:n], rq[:, 1, 0:n], rq[:, 1, 0:n], ALU.mult))
                link(dve, "dve", dve.tensor_tensor(rq[:, 2, 0:n], rq[:, 2, 0:n], rq[:, 0, 0:n], ALU.mult))
                link(dve, "dve", dve.tensor_scalar(rq[:, 2, 0:n], rq[:, 2, 0:n], -0.5, 1.5, ALU.mult, ALU.add))
                dve.tensor_tensor(rq[:, 3 + w, 0:n], rq[:, 1, 0:n], rq[:, 2, 0:n], ALU.mult).then_inc(hs_rstd, 1)
                dve.wait_ge(hs_rstd, 2 * b + w + 1)

        def spread_pe(pe, b, h):
            n = head_cols(b).stop - head_cols(b).start
            u = HEADS * b + h
            if u:
                pe.wait_ge(hs_done, u)
            for w in range(2):
                if h == 0:
                    pe.wait_ge(hs_rstd, 2 * b + w + 1)
                mm = pe.matmul(spread_bank(b, w), sel[:, h, :], rq[:, 3 + w, 0:n], start=True, stop=True)
            mm.then_inc(hs_bc, 1)

        def spread_bank(b, w):
            return ps[:, 4 + w, 0:T] if b else ps[:, 4, SEQ * w:SEQ * w + SEQ]

        def normed_dve(dve, b, h):
            cols = head_cols(b)
            dve.wait_ge(hs_bc, HEADS * b + h + 1)
            for w in range(2):
                x = proj[:, 8 + 8 * w + h, cols]
                ins = dve.scalar_tensor_tensor(out=x, in0=x, scalar=qk_gain[:, 2 * b + w:2 * b + w + 1], in1=spread_bank(b, w),
                                               op0=ALU.mult, op1=ALU.mult)
            ins.then_inc(hs_done, 1)

        block = nc.Block()
        with block:
            SSM_IN = 16 * 8
            SSM_ITERS = SSM_TILES // 4

            def is_first(i):
                return isinstance(i, int) and i == 0

            def is_last(i):
                return isinstance(i, int) and i == SSM_ITERS - 1

            def pairs(eng, body):
                def both(k):
                    for parity in range(2):
                        body(2 * k + parity, parity)
                both(0)
                loop(eng, 1, SSM_ITERS // 2 - 1, both)
                both(SSM_ITERS // 2 - 1)

            @block.sync
            def _(sp):
                for r, nm in enumerate(("ssm_a_re", "ssm_a_im")):
                    sp.dma_start(pre[:, r, :], a[nm][0].rearrange("(t g) n -> t (g n)", g=2)).then_inc(mix_in, 16)
                sp.dma_start(ldt[:, 0:2], a["ssm_log_dt"][0].rearrange("(t g) -> t g", g=2)).then_inc(mix_in, 16)
                sp.dma_start(steps[:, :], a["steps"]).then_inc(mix_in, 16)
                for r, nm in enumerate(("ssm_b_re", "ssm_b_im")):
                    sp.dma_start(b_nat[:, r, :, :], a[nm][0].rearrange("(t g) n c -> (g n) t c", g=2)).then_inc(mix_in, 16)
                for r, nm in enumerate(("ssm_c_re", "ssm_c_im")):
                    sp.dma_start(c_nat[:, r, :, :], a[nm][0].rearrange("(i g) c n -> (g c) i n", g=8)).then_inc(mix_in, 16)

            @block.gpsimd
            def _(pool):
                pool.memset(ebuf[:, :, :, :], 0.0).then_inc(pool_zero, 1)
                pool.memset(ct[:, :, :, :], 0.0).then_inc(pool_zero, 1)

                def body(i):
                    for jj in range(4):
                        b, tile = jj % 2, 4 * i + jj
                        pool.wait_ge(g_ready, tile + 1)
                        if not (isinstance(tile, int) and tile == 0):
                            pool.wait_ge(h_ready, tile)
                        pool.tensor_tensor(o1[:, :, :], gg[:, b, :, :], cs[:, b:b + 1, :].broadcast_to([P, 2, SEQ]), ALU.mult)
                        pool.tensor_tensor(o2[:, :, :], gg[:, b, ::-1, :], sn[:, b, :, :], ALU.mult).then_inc(pool_step, 1)
                        pool.wait_ge(pool_step, tile + 1)
                        if not (isinstance(tile, int) and tile < 2):
                            pool.wait_ge(y_mm, tile - 1)
                        pool.tensor_tensor(hh[:, b, :, :], o1[:, :, :], o2[:, :, :], ALU.subtract).then_inc(h_ready, 1)

                body(0)
                loop(pool, 1, SSM_ITERS, body)

            @block.scalar
            def _(act):
                heads_act(act, 0, "s")
                act.wait_ge(mix_in, SSM_IN)
                act.activation(ldt[:, 2:4], ldt[:, 0:2], ACT.Exp).then_inc(pre_act, 1)
                act.wait_ge(pre_dve, 1)
                act.activation(pre[:, 3, :], pre[:, 2, :], ACT.Exp).then_inc(pre_act, 1)
                act.activation(pre[:, 4, :], pre[:, 2, :], ACT.Tanh, scale=0.5).then_inc(pre_act, 1)
                act.wait_ge(pre_dve, 9)
                act.activation(pre[:, 16, :], pre[:, 7, :], ACT.Abs).then_inc(pre_act, 1)
                act.activation(pre[:, 8, :], pre[:, 7, :], ACT.Sin, scale=TWO_PI).then_inc(pre_act, 1)
                act.activation(pre[:, 10, :], pre[:, 7, :], ACT.Sin, scale=TWO_PI / 2).then_inc(pre_act, 1)
                act.wait_ge(pre_act, 6)
                act.activation(pre[:, 9, :], pre[:, 16, :], ACT.Sin, scale=-TWO_PI, bias=half_pi[0:32, :]).then_inc(pre_act, 1)
                act.wait_ge(par_t, 1)
                act.activation(par[:, :, :], ps[:, 5, 0:P].rearrange("p (a t) -> p a t", a=4), ACT.Copy).then_inc(pre_act, 1)
                act.wait_ge(pool_zero, 2)
                act.wait_ge(pre_dve, 9 + 17 + 6)

                def tables(i, jj):
                    b, tile = jj % 2, 4 * i + jj
                    act.wait_ge(fr_ready, tile + 1)
                    if not (isinstance(tile, int) and tile < 2):
                        act.wait_ge(pool_step, tile - 1)
                    act.activation(sn[:, b, 0, :], fr[:, b, :], ACT.Sin, scale=TWO_PI)
                    act.activation(sn[:, b, 1, :], fr[:, b, :], ACT.Sin, scale=-TWO_PI)
                    act.activation(kk[:, b, :], fr[:, b, :], ACT.Abs).then_inc(tab_step, 1)
                    act.wait_ge(tab_step, tile + 1)
                    act.activation(cs[:, b, :], kk[:, b, :], ACT.Sin, scale=-TWO_PI, bias=half_pi[:, :]).then_inc(tab_ready, 1)

                def spread(i):
                    four = bass.ds(4 * i, 4) if not isinstance(i, int) else slice(4 * i, 4 * i + 4)
                    one = bass.ds(i, 1) if not isinstance(i, int) else slice(i, i + 1)
                    for r in range(2):
                        act.activation(ebuf[0:64, r, :, 0:16], bb[0:64, r, four, :], ACT.Copy)
                        act.activation(ebuf[64:P, r, :, 16:32], bb[64:P, r, four, :], ACT.Copy)
                        for d in range(2):
                            ins = act.activation(cd[:, r, d, :], c_nat[:, r, one, :].rearrange("p a n -> p (a n)"), ACT.Copy)
                    ins.then_inc(e_ready, 1)

                def transposed(i, parity):
                    act.wait_ge(bt_ps, i + 1)
                    act.activation(bt[:, parity, :, :], ps[:, 2, 0:2 * P].rearrange("p (a n) -> p a n", a=2), ACT.Copy).then_inc(bt_ready, 1)
                    act.wait_ge(ct_ps, i + 1)
                    if not (isinstance(i, int) and i < 2):
                        act.wait_ge(y_mm, 4 * (i - 1))
                    for r in range(2):
                        for half in range(2):
                            rows_ = slice(64 * half, 64 * half + 64)
                            cols_ = slice(16 * half, 16 * half + 16)
                            dst = ct[rows_, parity, r, :].rearrange("p (j q) -> p j q", q=160)[:, :, cols_]
                            src = ps[rows_, 3, P * r:P * r + P].rearrange("p (j q) -> p j q", q=32)[:, :, cols_]
                            ins = act.activation(dst, src, ACT.Copy, scale=(1.0, -1.0)[r])
                    ins.then_inc(ct_ready, 1)

                def body(i, parity):
                    for jj in range(4):
                        if jj < 2:
                            tables(i, jj + 2)
                        elif not is_last(i):
                            tables(i + 1, jj - 2)
                        if jj == 0 and not is_last(i):
                            spread(i + 1)
                        if jj == 1 and not is_last(i):
                            transposed(i + 1, 1 - parity)

                spread(0)
                transposed(0, 0)
                tables(0, 0)
                tables(0, 1)
                pairs(act, body)
                heads_act(act, 0, "r")
                act.wait_ge(y_ready, 8)
                for h in range(2):
                    act.activation(proj[:, 4 * h:4 * h + 4, SEQ_COLS], proj[:, 4 * h:4 * h + 4, SEQ_COLS],
                                   ACT.Gelu_apprx_tanh).then_inc(gelu_done, 1)

            @block.vector
            def _(dve):
                step = [0]

                def pstep(ins):
                    step[0] += 1
                    ins.then_inc(pre_dve, 1)
                    dve.wait_ge(pre_dve, step[0])

                def q(i):
                    return pre[:, i, :]

                def wide(x):
                    return x.rearrange("t (g o) -> t g o", o=1).broadcast_to([32, 2, STATES])

                dve.wait_ge(mix_in, SSM_IN)
                dve.wait_ge(pre_act, 1)
                pstep(dve.tensor_tensor(q(2).rearrange("t (g n) -> t g n", g=2), q(0).rearrange("t (g n) -> t g n", g=2), wide(ldt[:, 2:4]), ALU.mult))
                pstep(dve.tensor_tensor(q(5).rearrange("t (g n) -> t g n", g=2), q(1).rearrange("t (g n) -> t g n", g=2), wide(ldt[:, 2:4]), ALU.mult))
                pstep(dve.tensor_scalar(q(6), q(5), float(1 / (2 * np.pi)), MAGIC, ALU.mult, ALU.add))
                pstep(dve.tensor_scalar(q(6), q(6), -MAGIC, None, ALU.add))
                pstep(dve.scalar_tensor_tensor(out=q(7), in0=q(6), scalar=-PI_A, in1=q(5), op0=ALU.mult, op1=ALU.add))
                pstep(dve.scalar_tensor_tensor(out=q(7), in0=q(6), scalar=-PI_B, in1=q(7), op0=ALU.mult, op1=ALU.add))
                pstep(dve.scalar_tensor_tensor(out=q(7), in0=q(6), scalar=-PI_C, in1=q(7), op0=ALU.mult, op1=ALU.add))
                pstep(dve.tensor_scalar(q(7), q(7), float(1 / (2 * np.pi)), 0.5, ALU.mult, ALU.min))
                pstep(dve.tensor_scalar(q(7), q(7), -0.5, None, ALU.max))
                dve.wait_ge(pre_act, 7)
                pstep(dve.scalar_tensor_tensor(out=q(4), in0=q(3), scalar=1.0, in1=q(4), op0=ALU.add, op1=ALU.mult))
                pstep(dve.tensor_tensor(q(11), q(4), q(9), ALU.mult))
                pstep(dve.tensor_tensor(q(16), q(10), q(10), ALU.mult))
                pstep(dve.scalar_tensor_tensor(out=q(11), in0=q(16), scalar=-2.0, in1=q(11), op0=ALU.mult, op1=ALU.add))
                pstep(dve.tensor_tensor(q(12), q(3), q(8), ALU.mult))
                pstep(dve.tensor_tensor(q(13), q(0), q(0), ALU.mult))
                pstep(dve.tensor_tensor(q(17), q(1), q(1), ALU.mult))
                pstep(dve.tensor_tensor(q(13), q(13), q(17), ALU.add))
                pstep(dve.reciprocal(q(13), q(13)))
                pstep(dve.tensor_tensor(q(14), q(11), q(0), ALU.mult))
                pstep(dve.tensor_tensor(q(16), q(12), q(1), ALU.mult))
                pstep(dve.tensor_tensor(q(14), q(14), q(16), ALU.add))
                pstep(dve.tensor_tensor(q(14), q(14), q(13), ALU.mult))
                pstep(dve.tensor_tensor(q(15), q(12), q(0), ALU.mult))
                pstep(dve.tensor_tensor(q(16), q(11), q(1), ALU.mult))
                pstep(dve.tensor_tensor(q(15), q(15), q(16), ALU.subtract))
                pstep(dve.tensor_tensor(q(15), q(15), q(13), ALU.mult))
                dve.wait_ge(mix_in, SSM_IN)
                dve.wait_ge(pre_act, 8)
                dve.wait_ge(mod_sum, 12)
                dve.tensor_tensor(mod[:, GATE1:GATE1 + 16], ps[:, 5, P:P + 16], bada[:, GATE1:GATE1 + 16], ALU.add)

                def z(i):
                    return par[:, i, :].rearrange("p (t o) -> p t o", o=1).broadcast_to([P, SSM_TILES, 16])

                pstep(dve.tensor_tensor(b_tmp[:, 0, :, :], b_nat[:, 0, :, :], z(2), ALU.mult))
                pstep(dve.tensor_tensor(b_tmp[:, 1, :, :], b_nat[:, 1, :, :], z(3), ALU.mult))
                pstep(dve.tensor_tensor(bb[:, 0, :, :], b_tmp[:, 0, :, :], b_tmp[:, 1, :, :], ALU.subtract))
                pstep(dve.tensor_tensor(b_tmp[:, 0, :, :], b_nat[:, 1, :, :], z(2), ALU.mult))
                pstep(dve.tensor_tensor(b_tmp[:, 1, :, :], b_nat[:, 0, :, :], z(3), ALU.mult))
                pstep(dve.tensor_tensor(bb[:, 1, :, :], b_tmp[:, 0, :, :], b_tmp[:, 1, :, :], ALU.add))
                assert step[0] == 32

                def turns(i, jj, parity):
                    b, tile = jj % 2, 4 * i + jj
                    dve.tensor_scalar(fr[:, b, :], steps[:, :], pc[:, parity, 0, jj:jj + 1], None, ALU.mult).then_inc(fr_step, 1)
                    dve.wait_ge(fr_step, 2 * tile + 1)
                    dve.tensor_scalar(kk[:, b, :], fr[:, b, :], MAGIC, -MAGIC, ALU.add, ALU.add).then_inc(fr_step, 1)
                    dve.wait_ge(fr_step, 2 * tile + 2)
                    dve.tensor_tensor(fr[:, b, :], fr[:, b, :], kk[:, b, :], ALU.subtract).then_inc(fr_ready, 1)

                def scan(i, jj, parity):
                    b, tile = jj % 2, 4 * i + jj
                    bu = ps[:, b, :].rearrange("p (a n) -> p a n", a=2)
                    dve.wait_ge(bu_ready, tile + 1)
                    dve.wait_ge(tab_ready, tile + 1)
                    dve.tensor_tensor(t1[:, :, :], bu, cs[:, b:b + 1, :].broadcast_to([P, 2, SEQ]), ALU.mult)
                    dve.tensor_tensor(t2[:, :, :], bu[:, ::-1, :], sn[:, b, :, :], ALU.mult).then_inc(rot_step, 1)
                    dve.wait_ge(rot_step, 2 * tile + 1)
                    if not (isinstance(tile, int) and tile == 0):
                        dve.wait_ge(g_ready, tile)
                    dve.tensor_tensor(vv[:, :, :], t1[:, :, :], t2[:, :, :], ALU.add).then_inc(rot_step, 1)
                    dve.wait_ge(rot_step, 2 * tile + 2)
                    if not (isinstance(tile, int) and tile < 2):
                        dve.wait_ge(pool_step, tile - 1)
                    for r in range(2):
                        ins = dve.tensor_tensor_scan(gg[:, b, r, :], pc[:, parity, 1, jj:jj + 1].broadcast_to([P, SEQ]), vv[:, r, :],
                                                     0.0, ALU.mult, ALU.add)
                    ins.then_inc(g_ready, 1)

                def y_out(i, parity):
                    dve.wait_ge(y_mm, 4 * i + 4)
                    u = tile_ap(proj, i, SEQ_COLS)
                    d = vecs[:, V_D + i:V_D + i + 1] if isinstance(i, int) else vecs[:, bass.ds(V_D + i, 1)]
                    dve.scalar_tensor_tensor(out=u, in0=u, scalar=d, in1=ps[:, 4 + 2 * parity, 0:SEQ], op0=ALU.mult, op1=ALU.add).then_inc(y_ready, 1)

                def fetch(i, parity):
                    four = bass.ds(4 * i, 4) if not isinstance(i, int) else slice(4 * i, 4 * i + 4)
                    dve.tensor_copy(pc[:, parity, :, :], par[:, 0:2, four])
                    dve.tensor_copy(ui[:, parity, :], tile_ap(proj, i, SEQ_COLS)).then_inc(ui_ready, 1)

                def body(i, parity):
                    for jj in range(4):
                        scan(i, jj, parity)
                        if jj < 2:
                            turns(i, jj + 2, parity)
                        elif not is_last(i):
                            if jj == 2:
                                dve.wait_ge(ui_ready, i + 2)
                            turns(i + 1, jj - 2, 1 - parity)
                        if jj == 0 and not is_last(i):
                            fetch(i + 1, 1 - parity)
                        if jj == 1 and not is_first(i):
                            y_out(i - 1, 1 - parity)

                fetch(0, 0)
                dve.wait_ge(ui_ready, 1)
                turns(0, 0, 0)
                turns(0, 1, 0)
                pairs(dve, body)
                heads_dve(dve, 0)
                y_out(SSM_ITERS - 1, 1)

            @block.tensor
            def _(pe):
                heads_pe(pe, 0)
                for g in range(4):
                    gather(pe, accg1[:, g, :], 5, P + 4 * g)
                pe.wait_ge(pre_dve, 26)
                for n, s_ in enumerate((7, 3, 14, 15)):
                    mm = pe.transpose(ps[:, 5, 32 * n:32 * n + 32], pre[:, s_, :], ident[0:32, 0:32])
                mm.then_inc(par_t, 1)

                def drive(i, jj, parity):
                    b, tile = jj % 2, 4 * i + jj
                    if not (isinstance(tile, int) and tile < 2):
                        pe.wait_ge(rot_step, 2 * (tile - 2) + 1)
                    rows_ = slice(32 * jj, 32 * jj + 32)
                    for r in range(2):
                        mm = pe.matmul(ps[:, b, SEQ * r:SEQ * r + SEQ], bt[rows_, parity, r, :], ui[rows_, parity, :],
                                       start=True, stop=True)
                    mm.then_inc(bu_ready, 1)

                def read_out(i, jj, parity):
                    b, tile = jj % 2, 4 * i + jj
                    pe.wait_ge(h_ready, tile + 1)
                    for r in range(2):
                        mm = pe.matmul(ps[:, 4 + 2 * parity, 0:SEQ], ct[:, parity, r, P * jj:P * jj + P], hh[:, b, r, :],
                                       start=(jj == 0 and r == 0), stop=(jj == 3 and r == 1))
                    mm.then_inc(y_mm, 1)

                def turned(i):
                    pe.wait_ge(e_ready, i + 1)
                    for r in range(2):
                        mm = pe.transpose(ps[:, 2, P * r:P * r + P], ebuf[:, r, :, :].rearrange("p j c -> p (j c)"), ident)
                    mm.then_inc(bt_ps, 1)
                    for r in range(2):
                        mm = pe.transpose(ps[:, 3, P * r:P * r + P], cd[:, r, :, :].rearrange("p d n -> p (d n)"), ident)
                    mm.then_inc(ct_ps, 1)

                def body(i, parity):
                    pe.wait_ge(ct_ready, i + 1)
                    if not (isinstance(i, int) and i < 2):
                        pe.wait_ge(y_ready, i - 1)
                    for jj in range(4):
                        if jj < 2:
                            drive(i, jj + 2, parity)
                        elif not is_last(i):
                            if jj == 2:
                                pe.wait_ge(bt_ready, i + 2)
                                pe.wait_ge(ui_ready, i + 2)
                            drive(i + 1, jj - 2, 1 - parity)
                        if jj == 0 and not is_last(i):
                            turned(i + 1)
                        read_out(i, jj, parity)

                turned(0)
                pe.wait_ge(bt_ready, 1)
                pe.wait_ge(ui_ready, 1)
                drive(0, 0, 0)
                drive(0, 1, 0)
                pairs(pe, body)

        def span(b, qt):
            return slice(META if b == 0 else 0, META + P * (qt + 1))

        VG = [4, 6]

        def v_groups(b):
            return [(4 * b + i, i // 2, 4 * (i % 2)) for i in range(VG[b])]

        def v_pe(pe, b):
            for g, kt, h0 in v_groups(b):
                if g >= 2:
                    pe.wait_ge(v_copied, g - 1)
                for h in range(h0, h0 + 4):
                    c = 128 * (h - h0)
                    if kt < 2:
                        mm = pe.transpose(ps[:, 6 + g % 2, c:c + P], proj[:, 24 + h, META + P * kt:META + P * kt + P], ident)
                    else:
                        mm = pe.transpose(ps[0:META, 6 + g % 2, c:c + P], proj[:, 24 + h, 0:META], ident)
                mm.then_inc(v_t, 1)

        def v_act(act, b):
            for g, kt, h0 in v_groups(b):
                act.wait_ge(v_t, g + 1)
                r = P if kt < 2 else META
                act.activation(vt[0:r, kt, h0:h0 + 4, :], ps[0:r, 6 + g % 2, :].rearrange("p (h n) -> p h n", h=4),
                               ACT.Copy).then_inc(v_copied, 1)

        def key_tiles(b, qt):
            first = 0 if b == 0 else META
            tiles = [(slice(first + P * k, first + P * k + P), P, k) for k in range(qt + 1)]
            return tiles + ([(slice(0, META), META, 2)] if b else [])

        def units_pe(pe, b, beside):
            def scores(i):
                h, qt = UNITS[i]
                u = 16 * b + i
                keys = span(b, qt)
                n = keys.stop - keys.start
                if u >= 2:
                    pe.wait_ge(logit, u - 1)
                qs = slice(META + P * qt, META + P * qt + P)
                mm = pe.matmul(ps[:, u % 2, 0:n], proj[:, 8 + h, qs], proj[:, 16 + h, keys], start=True, stop=(b == 0))
                if b:
                    mm = pe.matmul(ps[:, u % 2, 0:n], sel[:, h, :], fg[:, 3, keys], start=False, stop=True)
                mm.then_inc(score, 1)

            def turn(i):
                h, qt = UNITS[i]
                u = 16 * b + i
                pe.wait_ge(p_norm, u + 1)
                if u >= 2:
                    pe.wait_ge(p_copied, u - 1)
                for cols, r, k in key_tiles(b, qt):
                    mm = pe.transpose(ps[0:r, 2 + u % 2, P * k:P * k + P], pn[:, u % 2, cols], ident)
                mm.then_inc(p_t, 1)

            def weigh(i):
                h, qt = UNITS[i]
                u = 16 * b + i
                pe.wait_ge(p_copied, u + 1)
                if u >= 2:
                    pe.wait_ge(pv_free, u - 1)
                tiles = key_tiles(b, qt)
                for n, (cols, r, k) in enumerate(tiles):
                    mm = pe.matmul(ps[:, 6 + u % 2, 0:P], vt[0:r, k, h, :], pt[0:r, u % 2, P * k:P * k + P],
                                   start=(n == 0), stop=(n == len(tiles) - 1))
                mm.then_inc(pv, 1)

            spread_pe(pe, b, 0)
            pe.wait_ge(hs_done, HEADS * b + 1)
            scores(0)
            for s_ in range(len(UNITS) + 2):
                if s_ + 1 < len(UNITS):
                    if s_ % 2 == 0 and s_ // 2 + 1 < HEADS:
                        if b and s_:
                            pe.wait_ge(pm_val, s_ // 2)
                        spread_pe(pe, b, s_ // 2 + 1)
                    if s_ % 2:
                        pe.wait_ge(hs_done, HEADS * b + (s_ + 1) // 2 + 1)
                    scores(s_ + 1)
                if s_ == 2:
                    pe.wait_ge(v_copied, sum(VG[:b + 1]))
                if s_ >= 2:
                    weigh(s_ - 2)
                if 1 <= s_ <= len(UNITS):
                    turn(s_ - 1)
                beside(s_)

        def units_act(act, b, beside=nothing):
            for s_ in range(len(UNITS) + 2):
                if s_ < len(UNITS):
                    i = s_
                    h, qt = UNITS[i]
                    u = 16 * b + i
                    n = span(b, qt).stop - span(b, qt).start
                    act.wait_ge(negmax, u + 1)
                    if u >= 2:
                        act.wait_ge(p_norm, u - 1)
                    if b:
                        act.activation(ex[:, u % 2, 0:n], lg[:, u % 2, 0:n], ACT.Exp, bias=st[:, u % 2, 1:2],
                                       accum_out=st[:, u % 2, 2:3]).then_inc(expd, 1)
                    else:
                        act.activation(ex[:, u % 2, 0:n], lg[:, u % 2, 0:n], ACT.Exp, bias=st[:, u % 2, 1:2]).then_inc(expd, 1)
                beside(s_)
                if s_ >= 2:
                    i = s_ - 2
                    h, qt = UNITS[i]
                    u = 16 * b + i
                    act.wait_ge(pv, u + 1)
                    act.activation(act_hi[:, 8 + h, META + P * qt:META + P * qt + P], ps[:, 6 + u % 2, 0:P], ACT.Copy).then_inc(pv_hi, 1)
                if 1 <= s_ <= len(UNITS):
                    i = s_ - 1
                    h, qt = UNITS[i]
                    u = 16 * b + i
                    act.wait_ge(p_t, u + 1)
                    if u >= 2:
                        act.wait_ge(pv, u - 1)
                    w = P * (qt + 1)
                    ins = act.activation(pt[:, u % 2, 0:w], ps[:, 2 + u % 2, 0:w], ACT.Copy)
                    if b:
                        ins = act.activation(pt[0:META, u % 2, 2 * P:3 * P], ps[0:META, 2 + u % 2, 2 * P:3 * P], ACT.Copy)
                    ins.then_inc(p_copied, 1)

        def units_dve(dve, b, beside=nothing):
            normed_dve(dve, b, 0)
            for s_ in range(len(UNITS) + 3):
                if s_ < len(UNITS):
                    i = s_
                    h, qt = UNITS[i]
                    u = 16 * b + i
                    n = span(b, qt).stop - span(b, qt).start
                    x = lg[:, u % 2, 0:n]
                    dve.wait_ge(score, u + 1)
                    if b:
                        c0 = 0 if qt == 0 else META + P
                        dve.scalar_tensor_tensor(out=x, in0=ps[:, u % 2, 0:n], scalar=cq[:, qt, h:h + 1], in1=causal[:, c0:c0 + n],
                                                 op0=ALU.add, op1=ALU.add).then_inc(logit, 1)
                    else:
                        c0 = 0 if qt == 0 else P
                        dve.scalar_tensor_tensor(out=x, in0=dil[:, c0:c0 + n], scalar=-(2.0 ** -(h + 1)), in1=ps[:, u % 2, 0:n],
                                                 op0=ALU.mult, op1=ALU.add).then_inc(logit, 1)
                    dve.wait_ge(logit, u + 1)
                    link(dve, "dve", dve.tensor_reduce(st[:, u % 2, 0:1], x, AX_X, ALU.max))
                    dve.tensor_scalar(st[:, u % 2, 1:2], st[:, u % 2, 0:1], -1.0, None, ALU.mult).then_inc(negmax, 1)
                beside(s_)
                if 1 <= s_ <= len(UNITS):
                    i = s_ - 1
                    h, qt = UNITS[i]
                    u = 16 * b + i
                    n = span(b, qt).stop - span(b, qt).start
                    dve.wait_ge(expd, u + 1)
                    if u >= 2:
                        dve.wait_ge(p_t, u - 1)
                    e = ex[:, u % 2, 0:n]
                    if b == 0:
                        c0 = 3 * P if qt == 0 else 4 * P
                        link(dve, "dve", dve.scalar_tensor_tensor(out=e, in0=e, scalar=1.0, in1=dil[:, c0:c0 + n], op0=ALU.mult,
                                                                  op1=ALU.mult, accum_out=st[:, u % 2, 2:3]))
                    link(dve, "dve", dve.reciprocal(st[:, u % 2, 3:4], st[:, u % 2, 2:3]))
                    dve.tensor_scalar(pn[:, u % 2, 0:n], e, st[:, u % 2, 3:4], None, ALU.mult).then_inc(p_norm, 1)
                if s_ % 2 == 0 and s_ // 2 + 1 < HEADS:
                    normed_dve(dve, b, s_ // 2 + 1)
                if s_ >= 3:
                    i = s_ - 3
                    h, qt = UNITS[i]
                    u = 16 * b + i
                    dve.wait_ge(pv_hi, u + 1)
                    o = slice(META + P * qt, META + P * qt + P)
                    dve.tensor_tensor(act_lo[:, 8 + h, o], ps[:, 6 + u % 2, 0:P], act_hi[:, 8 + h, o].bitcast(F32),
                                      ALU.subtract).then_inc(pv_free, 1)

        block = nc.Block()
        with block:
            @block.sync
            def _(sp):
                sp.dma_start(sel[:, :, :], a["sel"].rearrange("a (h p) -> a h p", h=HEADS)).then_inc(mix_in, 16)
                sp.dma_start(dil[:, :], a["dilated"]).then_inc(mix_in, 16)
                stream(sp, "attn", head=False)
                stream(sp, "glu")

            @block.scalar
            def _(act):
                v_act(act, 0)
                units_act(act, 0)

            @block.vector
            def _(dve):
                dve.wait_ge(mix_in, SSM_IN + 32)
                p = byname["attn"]
                units_dve(dve, 0, lambda s_: condition(dve, p, 0, s_, accs2[:, s_ // 4, :], s_ % 4) if s_ < p.body else None)
                dve.wait_ge(mod_sum, 16)
                link(dve, "dve", dve.tensor_tensor(mod[:, SCALE2:SCALE2 + 16], ps[:, 5, 0:16], bada[:, SCALE2:SCALE2 + 16], ALU.add))
                link(dve, "dve", dve.tensor_scalar(gain[:, :], mod[:, SCALE2:SCALE2 + 16], 1.0, None, ALU.add))
                link(dve, "dve", dve.tensor_tensor(gain[:, :], gain[:, :], vecs[:, V_N2:V_N2 + 16], ALU.mult))

            @block.tensor
            def _(pe):
                pe.wait_ge(mix_in, SSM_IN + 32)
                v_pe(pe, 0)

                def conditioning(s_):
                    if s_ in (4, 8, 12, 16):
                        g = s_ // 4 - 1
                        pe.wait_ge(acc_step, CK * (byname["attn"].before["V"] + 4 * g + 4))
                        gather(pe, accs2[:, g, :], 5, 4 * g)

                units_pe(pe, 0, conditioning)

        y_lo = hid_hi[:, 8:16, :]
        MIX2 = SSM_IN + 16 * 7

        def glu_act(act, p, it, g):
            group_done(act, p, it, g)
            if g:
                act.wait_ge(glu_mul, g)
            act.activation(sig[:, :, 0:SEQ], bank(g, SEQ_COLS), ACT.Sigmoid).then_inc(bank_free[g], 1)

        def glu_dve(dve, p, it, g):
            dve.wait_ge(bank_free[g], group_index(p, it, g) + 1)
            s_ = slice(4 * g, 4 * g + 4)
            if g:
                dve.wait_ge(act_ready, ACT0["mix1"] + g)
            dve.tensor_tensor(val[:, :, 0:SEQ], sig[:, :, 0:SEQ], proj[:, s_, SEQ_COLS], ALU.mult).then_inc(glu_mul, 1)
            dve.wait_ge(glu_mul, g + 1)
            link(dve, "dve", dve.tensor_copy(act_hi[:, s_, SEQ_COLS], val[:, :, 0:SEQ]))
            dve.tensor_tensor(act_lo[:, s_, SEQ_COLS], val[:, :, 0:SEQ], act_hi[:, s_, SEQ_COLS].bitcast(F32),
                              ALU.subtract).then_inc(act_ready, 1)

        def then(*fs):
            def run(*second):
                for f in fs[:-1]:
                    if f:
                        f()
                fs[-1](*second)
            return run

        block = nc.Block()
        with block:
            @block.sync
            def _(sp):
                stream(sp, "w_out")
                for f in ("ffn1", "ffn2"):
                    for i in range(len(PARTS)):
                        stream(sp, f"{f}.up{i}")
                        stream(sp, f"{f}.down{i}")
                stream(sp, "w_in_2")
                sp.wait_ge(act_ready, ACT0["mix_2"] + QUADS)
                sp.dma_start(sel[:, :, :], a["sel"].rearrange("a (h p) -> a h p", h=HEADS)).then_inc(mix_in, 16)
                sp.dma_start(causal[:, :], a["causal"]).then_inc(mix_in, 16)
                sp.dma_start(wf[:, :, :], a["w_in_2"][0][:, 4 * HALFW:4 * HALFW + HEADS].rearrange("(t p) n -> p t n", p=P)).then_inc(mix_in, 16)
                sp.dma_start(bf[:, :], a["b_forget_2"].rearrange("a h -> h a")).then_inc(mix_in, 16)
                sp.dma_start(pw[:, :, :, :], a["pool_w_2"][0].rearrange("g (k p) n -> p g k n", p=P)).then_inc(mix_in, 16)
                stream(sp, "w_out_2", rest=False)

            @block.scalar
            def _(act):
                pend = run_phase(act, "glu", split_hi, bind(act, glu_act), None)
                pend = run_phase(act, "w_out", split_hi, bind(act, squares_of(4)), pend)
                pend = ffn_act(act, "ffn1", then(pend, lambda: norm_act(act, "norm2", 48)), squares_of(8))
                pend = ffn_act(act, "ffn2", then(pend, lambda: norm_act(act, "ffn1_2")), squares_of(12))
                pend = run_phase(act, "w_in_2", split_hi, bind(act, copy_out), then(pend, lambda: norm_act(act, "mix_2")))
                pend()

            @block.vector
            def _(dve):
                dve.wait_ge(gelu_done, 2)
                for g in range(2):
                    hi, lo = slice(4 * g, 4 * g + 4), slice(8 + 4 * g, 12 + 4 * g)
                    link(dve, "dve", dve.tensor_copy(hid_hi[:, hi, SEQ_COLS], proj[:, hi, SEQ_COLS]))
                    dve.tensor_tensor(hid_hi[:, lo, SEQ_COLS], proj[:, hi, SEQ_COLS], hid_hi[:, hi, SEQ_COLS].bitcast(F32),
                                      ALU.subtract).then_inc(y_split, 1)
                pend = run_phase(dve, "glu", split_lo, bind(dve, glu_dve), None)
                gate1 = with_squares(4, add_dve(("mod", 32)))
                pend = run_phase(dve, "w_out", split_lo, bind(dve, gate1), pend, accb2)

                def shift2():
                    dve.wait_ge(mod_sum, 20)
                    dve.tensor_tensor(mod[:, SHIFT2:SHIFT2 + 16], ps[:, 1, 0:16], bada[:, SHIFT2:SHIFT2 + 16], ALU.add)

                pend = ffn_dve(dve, "ffn1", then(pend, shift2, lambda second: norm_dve(dve, "norm2", gain, 0, 48, second)), add_dve(("mod", 80)),
                               with_squares(8, add_dve(("mod", 80))))
                pend = ffn_dve(dve, "ffn2", then(pend, lambda second: norm_dve(dve, "ffn1_2", vecs, V_F1, None, second)), add_dve(("const", 0.5)),
                               with_squares(12, add_dve(("const", 0.5))))
                pend = run_phase(dve, "w_in_2", split_lo, nothing, then(pend, lambda second: norm_dve(dve, "mix_2", vecs, V_MIX, None, second)), norm=True)

            @block.tensor
            def _(pe):
                products(pe, "glu", hid_hi, y_lo, SEQ_COLS, lambda c: (y_split, c + 1))
                products(pe, "w_out", act_hi, act_lo, SEQ_COLS, lambda c: (act_ready, ACT0["mix1"] + c + 1) if c < 2 else None)
                p = byname["w_out"]
                pe.wait_ge(bank_free[0], group_index(p, 1, 0) + 1)
                for g in range(4):
                    pe.wait_ge(acc_step, CK * (p.before["V"] + 4 * g + 4))
                    gather(pe, accb2[:, g, :], 1, 4 * g)
                norm_pe(pe, "norm2")
                ffn_pe(pe, "ffn1", ACT0["norm2"])
                norm_pe(pe, "ffn1_2")
                ffn_pe(pe, "ffn2", ACT0["ffn1_2"])
                norm_pe(pe, "mix_2")
                products(pe, "w_in_2", act_hi, act_lo, slice(0, T), counted(act_ready, ACT0["mix_2"]))

            @block.gpsimd
            def _(pool):
                p = byname["w_in_2"]
                pool.wait_ge(act_ready, ACT0["mix_2"] + QUADS)
                for half in range(2):
                    pool.wait_ge(bank_free[half], group_index(p, 0, half) + 1)
                for g in range(4):
                    x = proj[:, 2 * g:2 * g + 2, :]
                    src = x
                    for l in range(g + 1):
                        w = 2 ** (l + 1)
                        dst = win[:, l % 2, :, :]
                        link(pool, "pool", pool.tensor_tensor(dst[:, :, w - 1:T], src[:, :, w - 1:T], src[:, :, w // 2 - 1:T - w // 2], ALU.add))
                        src = dst
                    link(pool, "pool", pool.tensor_scalar(src[:, :, SEQ_COLS], src[:, :, SEQ_COLS], 1.0 / 2 ** (g + 1), None, ALU.mult))
                    pool.tensor_tensor(x[:, :, SEQ_COLS], src[:, :, SEQ_COLS], x[:, :, SEQ_COLS], ALU.subtract).then_inc(pooled, 1)
                    pool.wait_ge(pooled, g + 1)

        block = nc.Block()
        with block:
            @block.scalar
            def _(act):
                act.wait_ge(mix_in, MIX2)
                act.activation(wf_hi[:, :, :], wf[:, :, :], ACT.Copy).then_inc(wf_split, 1)
                heads_act(act, 1)
                v_act(act, 1)
                act.wait_ge(fg_step, 1)
                act.activation(fg[:, 1, :], fg[:, 0, :], ACT.Abs).then_inc(act_link, 1)
                act.wait_ge(act_link, 1)
                act.activation(fg[:, 1, :], fg[:, 1, :], ACT.Exp, scale=-1.0).then_inc(act_link, 1)
                act.wait_ge(act_link, 2)
                act.activation(fg[:, 1, :], fg[:, 1, :], ACT.Ln, bias=1.0).then_inc(act_link, 1)
                act.wait_ge(cq_t, 1)
                act.activation(cq[:, :, :], ps[:, 5, 0:2 * HEADS].rearrange("p (t h) -> p t h", t=2), ACT.Copy).then_inc(cq_ready, 1)

                def pool_scaled(s_):
                    if s_ % 2 and s_ // 2 < HEADS:
                        o = s_ // 2
                        act.wait_ge(pmm, o + 1)
                        if o:
                            act.wait_ge(pm_free, o)
                        act.activation(pmix[:, :], ps[:, 4, 0:SEQ], ACT.Copy, scale=vecs[:, V_PS + o:V_PS + o + 1]).then_inc(pm_val, 1)

                units_act(act, 1, pool_scaled)

            @block.vector
            def _(dve):
                dve.wait_ge(wf_split, 1)
                dve.tensor_tensor(wf_lo[:, :, :], wf[:, :, :], wf_hi[:, :, :].bitcast(F32), ALU.subtract).then_inc(wf_split, 1)
                heads_dve(dve, 1)
                dve.wait_ge(fg_mm, 1)
                dve.tensor_scalar(fg[:, 0, :], ps[0:HEADS, 4, 0:T], bf[:, 0:1], None, ALU.add).then_inc(fg_step, 1)
                dve.wait_ge(act_link, 3)
                link(dve, "dve", dve.scalar_tensor_tensor(out=fg[:, 0, :], in0=fg[:, 0, :], scalar=0.0, in1=fg[:, 1, :], op0=ALU.min, op1=ALU.subtract))
                dve.tensor_tensor_scan(fg[:, 2, :], ones[0:HEADS, 0:1].broadcast_to([HEADS, T]), fg[:, 0, :], 0.0, ALU.mult, ALU.add).then_inc(fg_step, 1)
                dve.wait_ge(fg_step, 2)
                dve.tensor_scalar(fg[:, 3, :], fg[:, 2, :], -1.0, None, ALU.mult).then_inc(fg_step, 1)
                dve.wait_ge(mix_in, MIX2)
                dve.wait_ge(cq_ready, 1)

                def pool_split(s_):
                    if s_ % 2 == 0 and 1 <= s_ // 2 <= HEADS:
                        o = s_ // 2 - 1
                        dve.wait_ge(pm_val, o + 1)
                        link(dve, "dve", dve.tensor_copy(act_hi[:, o, SEQ_COLS], pmix[:, :]))
                        dve.tensor_tensor(act_lo[:, o, SEQ_COLS], pmix[:, :], act_hi[:, o, SEQ_COLS].bitcast(F32), ALU.subtract).then_inc(pm_free, 1)

                units_dve(dve, 1, pool_split)

            @block.tensor
            def _(pe):
                pe.wait_ge(wf_split, 2)
                for k in range(KT):
                    for w, x in ((wf_hi, act_hi), (wf_hi, act_lo), (wf_lo, act_hi)):
                        mm = pe.matmul(ps[0:HEADS, 4, 0:T], w[:, k, :], x[:, k, :],
                                       start=(k == 0 and x is act_hi and w is wf_hi), stop=(k == KT - 1 and w is wf_lo))
                mm.then_inc(fg_mm, 1)
                heads_pe(pe, 1)
                v_pe(pe, 1)
                pe.wait_ge(fg_step, 2)
                for qt in range(2):
                    mm = pe.transpose(ps[:, 5, HEADS * qt:HEADS * qt + HEADS], fg[:, 2, META + P * qt:META + P * qt + P], ident[0:HEADS, 0:HEADS])
                mm.then_inc(cq_t, 1)
                pe.wait_ge(fg_step, 3)
                pe.wait_ge(cq_ready, 1)

                def pool_mix(s_):
                    if s_ % 2 and s_ // 2 < HEADS:
                        o = s_ // 2
                        g, m = divmod(o, 2)
                        pe.wait_ge(pooled, g + 1)
                        if o:
                            pe.wait_ge(pm_val, o)
                        for k in range(2):
                            mm = pe.matmul(ps[:, 4, 0:SEQ], pw[:, g, k, P * m:P * m + P], proj[:, 2 * g + k, SEQ_COLS],
                                           start=(k == 0), stop=(k == 1))
                        mm.then_inc(pmm, 1)

                units_pe(pe, 1, pool_mix)

        block = nc.Block()
        with block:
            @block.sync
            def _(sp):
                stream(sp, "w_out_2", head=False)
                for i in range(len(PARTS)):
                    stream(sp, f"ffn3.up{i}")
                    stream(sp, f"ffn3.down{i}")
                for n in range(8):
                    h, g = divmod(n, 4)
                    sp.wait_ge(out_copied, n + 1)
                    sp.dma_start(out[0, P * h:P * h + P, GROUP * g:GROUP * g + GROUP], outb[:, h, GROUP * g:GROUP * g + GROUP]).then_inc(out_done, 16)
                sp.wait_ge(out_done, 16 * 8)

            @block.scalar
            def _(act):
                pend = run_phase(act, "w_out_2", split_hi, bind(act, squares_of(16)), None)
                pend = ffn_act(act, "ffn3", then(pend, lambda: norm_act(act, "ffn2_2")), nothing)
                pend()
                for n in range(8):
                    h, g = divmod(n, 4)
                    act.wait_ge(out_t, n + 1)
                    act.activation(outb[:, h, GROUP * g:GROUP * g + GROUP], ps[:, n, :], ACT.Copy).then_inc(out_copied, 1)

            @block.vector
            def _(dve):
                pend = run_phase(dve, "w_out_2", split_lo, bind(dve, with_squares(16, add_dve(("const", 1.0)))), None)
                pend = ffn_dve(dve, "ffn3", then(pend, lambda second: norm_dve(dve, "ffn2_2", vecs, V_F2, None, second)), add_dve(("const", 0.5)), add_dve(("const", 0.5)))
                pend()

            @block.tensor
            def _(pe):
                products(pe, "w_out_2", act_hi, act_lo, SEQ_COLS, lambda c: None)
                norm_pe(pe, "ffn2_2")
                ffn_pe(pe, "ffn3", ACT0["ffn2_2"])
                last = byname["ffn3.down2"]
                for half in range(2):
                    pe.wait_ge(bank_free[half], 1 + last.g1 // 2)
                for n in range(8):
                    h, g = divmod(n, 4)
                    for m in range(4):
                        mm = pe.transpose(ps[:, n, P * m:P * m + P], res[:, 4 * g + m, META + P * h:META + P * h + P], ident)
                    mm.then_inc(out_t, 1)


INPUTS = [
    "x", "c", "w_ada", "b_ada", "norm1_w", "w_in", "ssm_a_re", "ssm_a_im", "ssm_log_dt", "ssm_b_re", "ssm_b_im",
    "ssm_c_re", "ssm_c_im", "ssm_d", "ssm_w_glu", "q_norm_w", "k_norm_w", "w_out", "norm2_w", "w_ffn_gate",
    "w_ffn_up", "w_ffn_down", "meta_tokens_2", "ffn1_norm_2", "ffn1_w_gate_2", "ffn1_w_up_2", "ffn1_w_down_2",
    "mix_norm_2", "w_in_2", "b_forget_2", "q_norm_2", "k_norm_2", "pool_w_2", "pool_scale_2", "w_out_2",
    "ffn2_norm_2", "ffn2_w_gate_2", "ffn2_w_up_2", "ffn2_w_down_2",
]


def kernel(**inputs):
    import concourse.bacc as bacc
    from concourse.bass_utils import run_bass_kernel_spmd

    nc = bacc.Bacc("TRN2", target_bir_lowering=False, num_devices=1)
    arrays = {n: np.ascontiguousarray(inputs[n]) for n in INPUTS}
    arrays.update(constants())
    aps = {n: nc.dram_tensor(f"in_{n}", v.shape, mybir.dt.from_np(v.dtype), kind="ExternalInput").ap() for n, v in arrays.items()}
    out = nc.dram_tensor("out_x", (1, SEQ, D), F32, kind="ExternalOutput").ap()
    build(nc, aps, out)
    run = run_bass_kernel_spmd(nc, [{f"in_{n}": v for n, v in arrays.items()}], core_ids=[0])
    return run.results[0]["out_x"]
```
